# Optimizing a Trainium2 kernel written in Bass

```python
import jax, jax.numpy as jnp
from jax import lax
import numpy as np

D_MODEL = 2048
BATCH = 1
SEQ = 512
DEPTH = 1

HEAD_DIM = 64
N_HEADS_A = 16
N_HEADS_B = 16
N_KV_B = 2
REP_B = N_HEADS_B // N_KV_B
D_A = N_HEADS_A * HEAD_DIM
D_B = N_HEADS_B * HEAD_DIM
D_KV_B = N_KV_B * HEAD_DIM
D_MIX = D_A + D_B
IN_COLS = 3 * D_A + D_B + 2 * D_KV_B
N_ALIBI = N_HEADS_A + N_HEADS_B
DILATED_CFG = ((128, 1), (512, 4), (2048, 16))
SWA_WINDOW = 128
BLK = 128
D_FF = -(-(8 * D_MODEL) // (3 * 256)) * 256
EPS = 1e-6

kernel_name = "hybrid_dilated_swa_sink_alibi"

def rmsnorm(x, g):
    xf = x.astype(jnp.float32)
    y = xf * lax.rsqrt(jnp.mean(xf * xf, axis=-1, keepdims=True) + EPS)
    return (y * g.astype(jnp.float32)).astype(x.dtype)

def alibi_slopes():
    idx = jnp.arange(N_ALIBI, dtype=jnp.float32)
    s = jnp.exp2(-8.0 * (idx + 1.0) / N_ALIBI)
    return s[0::2], s[1::2]

def banded_parts(q, k, v, slopes, max_dist, pos_scale):
    n, g, r, L, dh = q.shape
    nb = -(-L // BLK)
    pad = nb * BLK - L
    q = jnp.pad(q, ((0, 0), (0, 0), (0, 0), (0, pad), (0, 0)))
    k = jnp.pad(k, ((0, 0), (0, 0), (BLK, pad), (0, 0)))
    v = jnp.pad(v, ((0, 0), (0, 0), (BLK, pad), (0, 0)))
    qb = q.reshape(n, g, r, nb, BLK, dh)
    kb = k.reshape(n, g, nb + 1, BLK, dh)
    vb = v.reshape(n, g, nb + 1, BLK, dh)
    kw = jnp.concatenate([kb[:, :, :-1], kb[:, :, 1:]], axis=3)
    vw = jnp.concatenate([vb[:, :, :-1], vb[:, :, 1:]], axis=3)
    scores = jnp.einsum('ngrbqd,ngbkd->ngrbqk', qb, kw).astype(jnp.float32) * (dh ** -0.5)
    qi = jnp.arange(BLK)[:, None]
    ki = jnp.arange(2 * BLK)[None, :]
    dist = qi + BLK - ki
    key_pos = jnp.arange(nb)[:, None, None] * BLK + ki[None] - BLK
    valid = (dist >= 0) & (dist <= max_dist) & (key_pos >= 0)
    bias = -slopes.astype(jnp.float32)[:, :, None, None, None] * (dist * pos_scale).astype(jnp.float32)
    logits = jnp.where(valid, scores + bias, -jnp.inf)
    m = jnp.max(logits, axis=-1, keepdims=True)
    p = jnp.exp(logits - m)
    s = jnp.sum(p, axis=-1, keepdims=True)
    num = jnp.einsum('ngrbqk,ngbkd->ngrbqd', p, vw.astype(jnp.float32))
    num = num.reshape(n, g, r, nb * BLK, dh)[:, :, :, :L]
    m = m.reshape(n, g, r, nb * BLK, 1)[:, :, :, :L]
    s = s.reshape(n, g, r, nb * BLK, 1)[:, :, :, :L]
    return num, m, s

def dilated_attention(q, k, v, slopes):
    b, h, s_len, dh = q.shape
    nums, ms, ss = [], [], []
    for window, d in DILATED_CFG:
        ls = s_len // d

        def to_sub(t):
            return t.reshape(b, h, ls, d, dh).transpose(3, 0, 1, 2, 4).reshape(d * b, h, ls, dh)

        def from_sub(t):
            c = t.shape[-1]
            return t[:, :, 0].reshape(d, b, h, ls, c).transpose(1, 2, 3, 0, 4).reshape(b, h, s_len, c)

        num, m, sm = banded_parts(to_sub(q)[:, :, None], to_sub(k), to_sub(v),
                                  slopes[:, None], window // d, d)
        nums.append(from_sub(num))
        ms.append(from_sub(m))
        ss.append(from_sub(sm))
    m_all = jnp.maximum(jnp.maximum(ms[0], ms[1]), ms[2])
    w = [jnp.exp(mi - m_all) for mi in ms]
    numer = nums[0] * w[0] + nums[1] * w[1] + nums[2] * w[2]
    denom = ss[0] * w[0] + ss[1] * w[1] + ss[2] * w[2]
    return numer / denom

def swa_sink_attention(q, k, v, slopes, sinks):
    num, m, s = banded_parts(q, k, v, slopes, SWA_WINDOW - 1, 1)
    sink = sinks.astype(jnp.float32)[None, :, :, None, None]
    m2 = jnp.maximum(m, sink)
    c = jnp.exp(m - m2)
    return (num * c) / (s * c + jnp.exp(sink - m2))

def setup_inputs(seed: int = 0) -> dict:
    key = jax.random.key(seed)
    ks = jax.random.split(key, 12)
    f32 = jnp.float32
    x = jax.random.normal(ks[0], (BATCH, SEQ, D_MODEL), f32)
    attn_norm = 1.0 + 0.05 * jax.random.normal(ks[1], (DEPTH, D_MODEL), f32)
    w_in = jax.random.normal(ks[2], (DEPTH, D_MODEL, IN_COLS), f32) * D_MODEL ** -0.5
    sinks = 0.5 * jax.random.normal(ks[3], (DEPTH, N_HEADS_B), f32)
    out_norm_a = 1.0 + 0.05 * jax.random.normal(ks[4], (DEPTH, D_A), f32)
    out_norm_b = 1.0 + 0.05 * jax.random.normal(ks[5], (DEPTH, D_B), f32)
    w_out = jax.random.normal(ks[6], (DEPTH, D_MIX, D_MODEL), f32) * D_MIX ** -0.5
    ffn_norm = 1.0 + 0.05 * jax.random.normal(ks[7], (DEPTH, D_MODEL), f32)
    w_gate = jax.random.normal(ks[8], (DEPTH, D_MODEL, D_FF), f32) * D_MODEL ** -0.5
    w_up = jax.random.normal(ks[9], (DEPTH, D_MODEL, D_FF), f32) * D_MODEL ** -0.5
    w_down = jax.random.normal(ks[10], (DEPTH, D_FF, D_MODEL), f32) * D_FF ** -0.5
    final_norm = 1.0 + 0.05 * jax.random.normal(ks[11], (D_MODEL,), f32)
    return {"x": x, "attn_norm": attn_norm, "w_in": w_in, "sinks": sinks,
            "out_norm_a": out_norm_a, "out_norm_b": out_norm_b, "w_out": w_out,
            "ffn_norm": ffn_norm, "w_gate": w_gate, "w_up": w_up, "w_down": w_down,
            "final_norm": final_norm}

def reference(x, attn_norm, w_in, sinks, out_norm_a, out_norm_b, w_out,
              ffn_norm, w_gate, w_up, w_down, final_norm):
    b, s_len, _ = x.shape
    slopes_a, slopes_b = alibi_slopes()
    slopes_b = slopes_b.reshape(N_KV_B, REP_B)
    for l in range(DEPTH):
        h = rmsnorm(x, attn_norm[l])
        proj = jnp.einsum('bsd,de->bse', h, w_in[l])
        c0, c1, c2 = D_A, 2 * D_A, 3 * D_A
        c3, c4 = c2 + D_B, c2 + D_B + D_KV_B
        qa = proj[..., :c0].reshape(b, s_len, N_HEADS_A, HEAD_DIM).transpose(0, 2, 1, 3)
        ka = proj[..., c0:c1].reshape(b, s_len, N_HEADS_A, HEAD_DIM).transpose(0, 2, 1, 3)
        va = proj[..., c1:c2].reshape(b, s_len, N_HEADS_A, HEAD_DIM).transpose(0, 2, 1, 3)
        qb = proj[..., c2:c3].reshape(b, s_len, N_KV_B, REP_B, HEAD_DIM).transpose(0, 2, 3, 1, 4)
        kb = proj[..., c3:c4].reshape(b, s_len, N_KV_B, HEAD_DIM).transpose(0, 2, 1, 3)
        vb = proj[..., c4:].reshape(b, s_len, N_KV_B, HEAD_DIM).transpose(0, 2, 1, 3)

        out_a = dilated_attention(qa, ka, va, slopes_a)
        out_a = out_a.transpose(0, 2, 1, 3).reshape(b, s_len, D_A).astype(x.dtype)
        out_b = swa_sink_attention(qb, kb, vb, slopes_b, sinks[l].reshape(N_KV_B, REP_B))
        out_b = out_b.transpose(0, 3, 1, 2, 4).reshape(b, s_len, D_B).astype(x.dtype)
        mix = jnp.concatenate([rmsnorm(out_a, out_norm_a[l]),
                               rmsnorm(out_b, out_norm_b[l])], axis=-1)
        x = x + jnp.einsum('bse,ed->bsd', mix, w_out[l])
        h = rmsnorm(x, ffn_norm[l])
        gate = jnp.einsum('bsd,df->bsf', h, w_gate[l])
        up = jnp.einsum('bsd,df->bsf', h, w_up[l])
        x = x + jnp.einsum('bsf,fd->bsd', jax.nn.silu(gate) * up, w_down[l])
    return rmsnorm(x, final_norm)


_drawn_inputs = setup_inputs


def setup_inputs(seed=0):
    import zlib

    import numpy as np

    out = dict(_drawn_inputs(seed))
    spreads = {}
    factors = {}
    for name, (base, spread) in spreads.items():
        noise = np.random.default_rng([zlib.crc32(name.encode()), seed]).standard_normal(out[name].shape)
        drawn = base * np.exp(spread * noise) if base else spread * noise
        out[name] = __import__('jax').numpy.asarray(drawn.astype(out[name].dtype))
    for name, factor in factors.items():
        out[name] = (out[name] * factor).astype(out[name].dtype)
    return out
```

```python
import numpy as np

import concourse.bass as bass
from concourse import mybir
from concourse.alu_op_type import AluOpType as ALU

ACT = mybir.ActivationFunctionType
AX_X = mybir.AxisListType.X
F32 = mybir.dt.float32
F32R = mybir.dt.float32r
BYTES = 4

P = 128
SEQ = 512
D = 2048
DH = 64
HEADS = 16
D_A = HEADS * DH
D_KV = 2 * DH
IN_COLS = 3 * D_A + D_A + 2 * D_KV
FF = 5632
EPS = 1e-6
NT = SEQ // P
KD = D // P
NC = D // SEQ
PAIRS = HEADS // 2
RING = 4
AHEAD = RING - 1
UNIT = 512
WINDOW = 128
BIG = 1.0e30
FLOOR = 3.0e38

U_KVB = 0
U_PAIR = 8
U_OUT = U_PAIR + 16 * PAIRS
U_FFN = U_OUT + 64
STEPS_F = FF // SEQ
UNITS = U_FFN + 48 * STEPS_F

BANK_Q, BANK_K, BANK_V = 0, 1, 4
BANK_S = (2, 3)
BANK_PT, BANK_O = 5, 7
BANK_G = (0, 4, 6, 1)
BANK_X = (2, 3, 5, 7)
BANK_GATE, BANK_UP = (2, 5), (3, 7)

S_A = [(3, 2, 0, 0, 512, 768), (2, 3, 0, 0, 384, 384), (0, 3, 384, 0, 128, 0), (1, 2, 0, 0, 256, 128)]
S_B = [(0, 2, 0, 0, 128, 0), (1, 2, 128, 0, 256, 128), (2, 3, 0, 128, 256, 384), (3, 3, 256, 256, 256, 640)]
E_A = {b: (e, k0) for b, _, _, k0, _, e in S_A}
E_B = {b: (e, k0) for b, _, _, k0, _, e in S_B}
PT_A = [[(0, (0, 1, 2, 3), 0)], [(1, (1, 2, 3), 0), (3, (3,), 384)], [(2, (2, 3), 0)]]
PT_B = [[(0, (0, 1), 0), (1, (1, 2), 256)], [(2, (2, 3), 0), (3, (3,), 256)]]
ROUNDS = 10
HEAD = [("A", 0, 0), ("A", 1, 3), ("B", 0, 6), ("B", 1, 8)]


def build(nc, x, attn_norm, w_in, sinks, out_norm_a, out_norm_b, w_out, ffn_norm,
          w_gate, w_up, w_down, final_norm, c_dist, c_lnm, c_band, c_slope, c_ident, out):
    spot = [(nc.sbuf_base + 63) // 64 * 64]

    def sb(name, shape, dt=F32, at=None):
        place = spot[0] if at is None else at
        size = int(np.prod(shape[1:])) * BYTES
        t = nc.alloc_sbuf_tensor_at(name, shape, dt, offset=place)
        if at is None:
            spot[0] = place + (size + 31) // 32 * 32
        assert place + size <= nc.sbuf_usable_end, name
        ends[name] = place + size
        return t

    ends = {}
    ident = sb("ident", [P, P])
    ones = sb("ones", [P, P])
    gains = sb("gains", [P, 2 * KD + 2 * PAIRS])
    sink = sb("sink", [P, HEADS])
    neg_sink = sb("neg_sink", [P, HEADS])
    slope = sb("slope", [P, 2 * HEADS])
    half = sb("half", [P, 8])
    tick = sb("tick", [P, 20])
    sums = sb("sums", [P, NT, NC])
    total = sb("total", [P, NT])
    mean = sb("mean", [P, 8])
    inv = sb("inv", [P, 8])
    raw = sb("raw", [P, RING, UNIT])
    w_hi = sb("w_hi", [P, RING, UNIT], F32R)
    w_lo = sb("w_lo", [P, RING, UNIT], F32R)
    place_x = spot[0]
    h_hi = sb("h_hi", [P, KD, SEQ], F32R)
    place_y = spot[0]
    h_lo = sb("h_lo", [P, KD, SEQ], F32R)
    place_o = spot[0]
    o_t = sb("o_t", [P, 2 * PAIRS, SEQ])
    place_g = spot[0]
    act_hi = sb("act_hi", [P, 4, SEQ], F32R)
    act_lo = sb("act_lo", [P, 4, SEQ], F32R)
    kb_all = sb("kb_all", [P, SEQ], at=place_g)
    vb_all = sb("vb_all", [P, NT, P], at=place_g + 2048)
    x_first = sb("x_first", [P, NT, D], at=place_o)
    place_att = spot[0]
    proj = [sb(f"proj{i}", [P, SEQ]) for i in range(2)]
    q_hi = {"A": sb("qa_hi", [P, SEQ], F32R), "B": sb("qb_hi", [P, SEQ], F32R)}
    q_lo = {"A": sb("qa_lo", [P, SEQ], F32R), "B": sb("qb_lo", [P, SEQ], F32R)}
    k_hi = {"A": sb("ka_hi", [P, SEQ], F32R), "B": sb("kb_hi", [P, SEQ], F32R)}
    k_lo = {"A": sb("ka_lo", [P, SEQ], F32R), "B": sb("kb_lo", [P, SEQ], F32R)}
    v_hi = {"A": sb("va_hi", [P, NT, 4, DH], F32R), "B": sb("vb_hi", [P, NT, 4, DH], F32R)}
    v_lo = {"A": sb("va_lo", [P, NT, 4, DH], F32R), "B": sb("vb_lo", [P, NT, 4, DH], F32R)}
    dist = sb("dist", [P, SEQ])
    lnm = sb("lnm", [P, SEQ])
    band = sb("band", [P, 2 * P])
    bias = sb("bias", [P, SEQ])
    probs = [sb(f"probs{i}", [P, 10 * P]) for i in range(2)]
    pt_hi = sb("pt_hi", [P, 2, SEQ], F32R)
    pt_lo = sb("pt_lo", [P, 2, SEQ], F32R)
    squares = sb("squares", [P, SEQ])
    sq_sum = {"A": sb("sq_a", [P, SEQ]), "B": sb("sq_b", [P, SEQ])}
    r_bc = sb("r_bc", [P, SEQ])
    low = sb("low", [P, 16])
    den = sb("den", [P, 16])
    inv_den = sb("inv_den", [P, 16])
    sink_exp = sb("sink_exp", [P, 8])
    x_res = sb("x_res", [P, NT, D], at=place_x)
    y_a = sb("y_a", [P, NT, D], at=place_y)
    h2_lo = sb("h2_lo", [P, KD, SEQ], F32R, at=place_y)
    h2_hi = sb("h2_hi", [P, KD, SEQ], F32R, at=place_att)
    over = place_att + KD * SEQ * BYTES
    g_fin = sb("g_fin", [P, D], at=over)
    r2_bc = sb("r2_bc", [P, SEQ], at=over + 8192)
    r2_wide = sb("r2_wide", [P, NT, P], at=over + 10240)
    junk = sb("junk", [P, SEQ], at=over + 12288)
    gate_s = sb("gate_s", [P, SEQ], at=over + 14336)
    silu_s = sb("silu_s", [P, SEQ], at=over + 16384)
    up_s = sb("up_s", [P, SEQ], at=over + 18432)
    act_s = sb("act_s", [P, SEQ], at=over + 20480)

    bank = [nc.alloc_psum_tensor(f"bank{i}", [P, 512], F32) for i in range(8)]

    def sem(name):
        return nc.alloc_semaphore(name)

    raw_loaded = [sem(f"raw_loaded{i}") for i in range(RING)]
    w_hi_done, w_lo_done, w_used = sem("w_hi_done"), sem("w_lo_done"), sem("w_used")
    x_loaded = [sem(f"x_loaded{i}") for i in range(NC)]
    x_again = [sem(f"x_again{i}") for i in range(NC)]
    consts_loaded, ident_loaded, ones_done, gains_loaded = sem("consts_loaded"), sem("ident_loaded"), sem("ones_done"), sem("gains_loaded")
    xt_ready, xt_hi_done, xt_lo_done = sem("xt_ready"), sem("xt_hi_done"), sem("xt_lo_done")
    sq_done, total_done, mean_done, inv_done = sem("sq_done"), sem("total_done"), sem("mean_done"), sem("inv_done")
    wide_done, rbc_ready, rbc_done = sem("wide_done"), sem("rbc_ready"), sem("rbc_done")
    acc_taken, gains_turned, gains_done = sem("acc_taken"), sem("gains_turned"), sem("gains_done")
    qa_hi_done, qa_lo_done = sem("qa_hi_done"), sem("qa_lo_done")
    ka_hi_done, ka_lo_done = sem("ka_hi_done"), sem("ka_lo_done")
    qb_hi_done, qb_lo_done = sem("qb_hi_done"), sem("qb_lo_done")
    kb_hi_done, kb_lo_done = sem("kb_hi_done"), sem("kb_lo_done")
    vt_ready, va_hi_done, va_lo_done = sem("vt_ready"), sem("va_hi_done"), sem("va_lo_done")
    vbt_ready, vb_all_done = sem("vbt_ready"), sem("vb_all_done")
    vb_hi_done, vb_lo_done, zero_done = sem("vb_hi_done"), sem("vb_lo_done"), sem("zero_done")
    s_ready, bias_done, low_done, sunk = sem("s_ready"), sem("bias_done"), sem("low_done"), sem("sunk")
    exp_done, sink_done, den_done, inv_den_done = sem("exp_done"), sem("sink_done"), sem("den_done"), sem("inv_den_done")
    p_ready, pt_ready, pt_hi_done, pt_lo_done = sem("p_ready"), sem("pt_ready"), sem("pt_hi_done"), sem("pt_lo_done")
    pv_done, o_sq_done, o_taken, sq_added = sem("pv_done"), sem("o_sq_done"), sem("o_taken"), sem("sq_added")
    ssq_ready, act_hi_done, act_lo_done = sem("ssq_ready"), sem("act_hi_done"), sem("act_lo_done")
    grp_ready, grp_taken, y_done = sem("grp_ready"), sem("grp_taken"), sem("y_done")
    gu_ready, gu_taken, silu_done, act_done = sem("gu_ready"), sem("gu_taken"), sem("silu_done"), sem("act_done")
    neg_done, gfin_loaded = sem("neg_done"), sem("gfin_loaded")
    scaled, stored = sem("scaled"), sem("stored")

    w_in2, w_out2 = w_in[0], w_out[0]
    w_gate2, w_up2, w_down2 = w_gate[0], w_up[0], w_down[0]
    x2, out2 = x[0], out[0]
    gain_rows = probs[0]
    G_ATTN, G_FFN, G_OUT = 0, KD, 2 * KD

    block = nc.Block()
    block.__enter__()

    def col_in(kind, p):
        return {"q": 0, "k": D_A, "v": 2 * D_A, "qb": 3 * D_A}[kind] + p * P

    def ahead(v4, s):
        return (v4, AHEAD) if s == 0 else (v4 + 1, s - 1)

    def x_bank(k, base):
        return bank[(BANK_G if base and k >= KD - 4 else BANK_X)[k % 4]]

    def with_bank(blocks, i):
        return max(j for j, b in enumerate(blocks) if b[1] == blocks[i][1]) + 1

    def wait_group(eng, g, n, t, u4):
        if t < NT - 1:
            eng.wait_ge(grp_ready, 3 * (4 * g + n) + t + 1)
        else:
            eng.wait_ge(w_used, 4 * (u4 + n) + 4)

    @block.sync
    def _(sp):
        def load(u4, s, src, first=False):
            if not first:
                sp.wait_ge(w_lo_done, 4 * u4 - 3 + s)
            dst = raw[:, s, :]
            if len(src.shape) == 3:
                dst = dst.rearrange("p (k c) -> p k c", c=P)
            sp.dma_start(dst, src).then_inc(raw_loaded[s], 16)

        def tall(w, j, col):
            return w[512 * j:512 * (j + 1), bass.ds(col, P)].rearrange("(k p) c -> p k c", p=P)

        for j in range(4):
            load(0, j, tall(w_in2, j, 4 * D_A), first=True)
        for j in range(4):
            load(1, j, tall(w_in2, j, 4 * D_A + D_KV))
        with sp.Fori(0, PAIRS) as p:
            for c, kind in enumerate(("q", "k", "v", "qb")):
                for j in range(4):
                    load(U_PAIR // 4 + 4 * p + c, j, tall(w_in2, j, col_in(kind, p)))
        with sp.Fori(0, 4) as g:
            for n in range(NC):
                for k in range(4):
                    load(U_OUT // 4 + 4 * g + n, k, w_out2[bass.ds(g * 512 + P * k, P), 512 * n:512 * (n + 1)])
        with sp.Fori(0, STEPS_F) as i:
            for c in range(4):
                for h, w in enumerate((w_gate2, w_up2)):
                    for j in range(4):
                        load(U_FFN // 4 + 12 * i + 2 * c + h, j, tall(w, j, i * 512 + P * c))
            for n in range(NC):
                for k in range(4):
                    load(U_FFN // 4 + 12 * i + 8 + n, k,
                         w_down2[bass.ds(i * 512 + P * k, P), 512 * n:512 * (n + 1)])
        for t in range(NT):
            sp.wait_ge(scaled, t + 1)
            sp.dma_start(out2[P * t:P * (t + 1), :], x_res[:, t, :]).then_inc(stored, 16)
        sp.wait_ge(stored, 16 * NT)

    @block.tensor
    def _(pe):
        def three(out_ap, st_hi, st_lo, mv_hi, mv_lo, start, stop):
            nc.tensor.matmul(out_ap, st_hi, mv_hi, start=start, stop=False, skip_group_check=True)
            nc.tensor.matmul(out_ap, st_hi, mv_lo, start=False, stop=False, skip_group_check=True)
            return nc.tensor.matmul(out_ap, st_lo, mv_hi, start=False, stop=stop, skip_group_check=True)

        def turn_x(src, k, base):
            if base + k >= 4:
                pe.wait_ge(xt_lo_done, base + k - 3)
            b = x_bank(k, base)
            for t in range(NT):
                mm = nc.tensor.transpose(b[:, P * t:P * (t + 1)], src[:, t, P * k:P * (k + 1)], ident[:, :])
            mm.then_inc(xt_ready, 1)

        def spread_r(wide, count, b):
            pe.wait_ge(wide_done, count)
            for t in range(NT):
                mm = nc.tensor.matmul(bank[b][:, P * t:P * (t + 1)], wide[:, t, :], ident[:, :], start=True, stop=True)
            mm.then_inc(rbc_ready, 1)

        def tall_unit(u4, j, b, hh, hl):
            pe.wait_ge(w_lo_done, 4 * u4 + j + 1)
            for k in range(4):
                ws = slice(P * k, P * (k + 1))
                mm = three(bank[b][:, :], w_hi[:, j, ws], w_lo[:, j, ws], hh[:, 4 * j + k, :], hl[:, 4 * j + k, :],
                           j == 0 and k == 0, j == 3 and k == 3)
            mm.then_inc(w_used, 1)

        def wide_unit(u4, s, g, split):
            n, k = s // 4, s % 4
            pe.wait_ge(w_lo_done, 4 * (u4 + n) + k + 1)
            if n == 0:
                pe.wait_ge(act_lo_done, split + k + 1)
            for t in range(NT):
                ts, b = slice(P * t, P * (t + 1)), bank[BANK_G[t]]
                if k == 0 and not (isinstance(g, int) and g == 0 and n == 0):
                    pe.wait_ge(grp_taken, 16 * g + 4 * n + t - 3)
                if k == 0 and isinstance(g, int) and g == 0 and n == 0:
                    pe.wait_ge(acc_taken, 2 + 4 * PAIRS if BANK_G[t] == BANK_K else 1 + 4 * PAIRS)
                nc.tensor.matmul(b[:, :], act_hi[:, k, ts], w_hi[:, k, :], start=k == 0, stop=False, skip_group_check=True)
                nc.tensor.matmul(b[:, :], act_hi[:, k, ts], w_lo[:, k, :], start=False, stop=False, skip_group_check=True)
                mm = nc.tensor.matmul(b[:, :], act_lo[:, k, ts], w_hi[:, k, :], start=False, stop=k == 3, skip_group_check=True)
                if k == 3 and t < NT - 1:
                    mm.then_inc(grp_ready, 1)
            mm.then_inc(w_used, 1)

        def scores(a, h, blocks):
            kind, odd, _ = HEAD[h]
            rows = slice(DH * odd, DH * (odd + 1))
            for b, bk, c0, k0, keys, _ in blocks:
                qs, ks = slice(P * b, P * (b + 1)), slice(k0, k0 + keys)
                three(bank[bk][:, c0:c0 + keys], q_hi[kind][rows, qs], q_lo[kind][rows, qs],
                      k_hi[kind][rows, ks], k_lo[kind][rows, ks], True, True).then_inc(s_ready, 1)

        def turn_p(a, h, r):
            kind, _, r0 = HEAD[h]
            if r == 0:
                pe.wait_ge(p_ready, 16 * a + 4 * (h + 1))
            if not (isinstance(a, int) and a == 0 and r0 + r == 0):
                pe.wait_ge(pt_lo_done, ROUNDS * a + r0 + r)
            where = E_A if kind == "A" else E_B
            for kb, qbs, c0 in (PT_A if kind == "A" else PT_B)[r]:
                for n, qb in enumerate(qbs):
                    e, k0 = where[qb]
                    e += P * kb - k0
                    mm = nc.tensor.transpose(bank[BANK_PT][:, c0 + P * n:c0 + P * (n + 1)],
                                             probs[h % 2][:, e:e + P], ident[:, :])
            mm.then_inc(pt_ready, 1)

        def weigh_v(a, h, r):
            kind, odd, r0 = HEAD[h]
            rounds = PT_A if kind == "A" else PT_B
            pe.wait_ge(pt_lo_done, ROUNDS * a + r0 + r + 1)
            buf = (r0 + r) % 2
            for i, (kb, qbs, c0) in enumerate(rounds[r]):
                n = P * len(qbs)
                vh = v_hi[kind][:, kb, 2 * odd:2 * odd + 2, :].rearrange("p a d -> p (a d)")
                vl = v_lo[kind][:, kb, 2 * odd:2 * odd + 2, :].rearrange("p a d -> p (a d)")
                mm = three(bank[BANK_O][:, P * qbs[0]:P * qbs[0] + n], vh, vl,
                           pt_hi[:, buf, c0:c0 + n], pt_lo[:, buf, c0:c0 + n], odd == 0 and r == 0 and i == 0,
                           odd == 1 and r == len(rounds) - 1 and i == len(rounds[r]) - 1)
            mm.then_inc(pv_done, 1)

        def turn_v():
            for t in range(NT):
                mm = nc.tensor.transpose(bank[BANK_O][:, P * t:P * (t + 1)], proj[0][:, P * t:P * (t + 1)], ident[:, :])
            return mm

        def attend(s, a, kv):
            first = isinstance(a, int) and a == 0
            if s == 0:
                pe.wait_ge(qa_lo_done, a + 1)
                pe.wait_ge(ka_lo_done, a + 1)
                if not first:
                    pe.wait_ge(exp_done, 16 * a)
                scores(a, 0, S_A[:3])
            if s == 1:
                pe.wait_ge(exp_done, 16 * a + 1)
                scores(a, 0, S_A[3:])
            if s == 2:
                pe.wait_ge(acc_taken, 5 + 4 * a)
                if first:
                    pe.wait_ge(vb_all_done, 1)
                else:
                    pe.wait_ge(o_taken, 2 * a)
                    pe.wait_ge(o_sq_done, 2 * a)
                turn_v().then_inc(vt_ready, 1)
            if s == 3:
                pe.wait_ge(exp_done, 16 * a + 4)
                scores(a, 1, S_A[:3])
            if s == 4:
                pe.wait_ge(exp_done, 16 * a + 5)
                scores(a, 1, S_A[3:])
                turn_p(a, 0, 0)
            if s == 5:
                turn_p(a, 0, 1)
                pe.wait_ge(va_lo_done, a + 1)
                weigh_v(a, 0, 0)
            if s == 6:
                turn_p(a, 0, 2)
                weigh_v(a, 0, 1)
                pe.wait_ge(qb_lo_done, a + 1)
                pe.wait_ge(kb_lo_done, 2 * (kv + 1))
                pe.wait_ge(exp_done, 16 * a + 8)
                scores(a, 2, S_B)
            if s == 7:
                weigh_v(a, 0, 2)
            if s == 8:
                turn_p(a, 1, 0)
            if s == 9:
                turn_p(a, 1, 1)
                weigh_v(a, 1, 0)
                pe.wait_ge(exp_done, 16 * a + 12)
                scores(a, 3, S_B)
            if s == 10:
                turn_p(a, 1, 2)
                weigh_v(a, 1, 1)
            if s == 11:
                weigh_v(a, 1, 2)
                turn_p(a, 2, 0)
            if s == 12:
                turn_p(a, 2, 1)
            if s == 13:
                pe.wait_ge(o_taken, 2 * a + 1)
                pe.wait_ge(o_sq_done, 2 * a + 1)
                pe.wait_ge(vb_lo_done, 2 * (kv + 1))
                weigh_v(a, 2, 0)
                turn_p(a, 3, 0)
            if s == 14:
                weigh_v(a, 2, 1)
                turn_p(a, 3, 1)
            if s == 15:
                weigh_v(a, 3, 0)
                weigh_v(a, 3, 1)

        def pair(p, a, kv):
            for c, b in enumerate((BANK_Q, BANK_K, BANK_V, BANK_K)):
                if c == 0:
                    pe.wait_ge(acc_taken, 1 if a is None else 4 * p - 1)
                if c in (1, 3):
                    pe.wait_ge(acc_taken, 4 * p + c + 1)
                if c == 2 and a is not None:
                    pe.wait_ge(acc_taken, 4 * p + 1)
                for j in range(4):
                    tall_unit(U_PAIR // 4 + 4 * p + c, j, b, h_hi, h_lo)
                    if a is not None:
                        attend(4 * c + j, a, kv)
                    if a is None and c == 0 and j == 1:
                        pe.wait_ge(acc_taken, 2)
                        turn_v().then_inc(vbt_ready, 1)

        pe.wait_ge(ident_loaded, 16)
        pe.wait_ge(gains_loaded, 16 * 4)
        rows = 2 * KD + 2 * PAIRS
        nc.tensor.transpose(bank[BANK_Q][:, 0:rows], gain_rows[0:rows, 0:P], ident[0:rows, 0:rows]).then_inc(gains_turned, 1)
        for k in range(8):
            if k % 4 == 0:
                pe.wait_ge(x_loaded[k // 4], 16)
            turn_x(x_first, k, 0)
        pe.wait_ge(gains_done, 1)
        for s in range(8):
            if s < 4:
                pe.wait_ge(xt_lo_done, 4 * s + 4)
            tall_unit(s // 4, s % 4, (BANK_Q, BANK_K)[s // 4], h_hi, h_lo)
            if s < 2:
                pe.wait_ge(x_loaded[2 + s], 16)
                for k in range(8 + 4 * s, 12 + 4 * s):
                    turn_x(x_first, k, 0)
            if s == 5:
                pe.wait_ge(xt_lo_done, KD)
                spread_r(squares[:, :].rearrange("p (t c) -> p t c", c=P), 1, BANK_PT)
        pe.wait_ge(rbc_done, 1)
        pair(0, None, 0)
        pair(1, 0, 0)
        with pe.Fori(2, 5) as p:
            pair(p, p - 1, 0)
        with pe.Fori(5, PAIRS) as p:
            pair(p, p - 1, 1)

        for g in range(4):
            for s in range(16):
                wide_unit(U_OUT // 4 + 4 * g, s, g, 4 * g)
                if g == 0:
                    attend(s, PAIRS - 1, 1)
                if g == 1 and s == 1:
                    pe.wait_ge(sq_added, 2 * PAIRS)
                    pe.wait_ge(pt_lo_done, ROUNDS * PAIRS)
                    for i, kind in enumerate("AB"):
                        for t in range(NT):
                            mm = nc.tensor.matmul(bank[BANK_PT][:, 4 * i + t:4 * i + t + 1],
                                                  sq_sum[kind][:, P * t:P * (t + 1)], ones[:, 0:1], start=True, stop=True)
                    mm.then_inc(ssq_ready, 1)
                if g == 3 and s % 4 == 2 and s > 4:
                    n = s // 4 - 1
                    pe.wait_ge(grp_taken, 16 * g + 4 * n + 4)
                    for k in range(4 * n, 4 * n + 4):
                        turn_x(x_res, k, KD)

        def ffn(i, first):
            u = U_FFN // 4 + 12 * i
            for c in range(4):
                for h, banks in enumerate((BANK_GATE, BANK_UP)):
                    b = banks[c % 2]
                    if not first or c >= 2:
                        pe.wait_ge(gu_taken, 8 * i + 2 * c + h - 3)
                    elif b != BANK_X[3]:
                        pe.wait_ge(xt_lo_done, 2 * KD - 8 + BANK_X.index(b) + 1)
                    else:
                        pe.wait_ge(rbc_done, 2)
                    for j in range(4):
                        if first and c == 0 and h == 0:
                            pe.wait_ge(xt_lo_done, KD + 4 * j + 4)
                        tall_unit(u + 2 * c + h, j, b, h2_hi, h2_lo)
                        if first and c == 0 and h == 0 and j == 1:
                            pe.wait_ge(grp_taken, 64)
                            for k in range(12, KD):
                                turn_x(x_res, k, KD)
                        if first and c == 0 and h == 0 and j == 3:
                            pe.wait_ge(xt_lo_done, 2 * KD)
                            spread_r(r2_wide, 2, BANK_X[3])
            for s in range(16):
                wide_unit(u + 8, s, 4 + i, 16 + 4 * i)

        ffn(0, True)
        with pe.Fori(1, STEPS_F) as i:
            ffn(i, False)

    @block.scalar
    def _(act):
        def split(u4, s, wait_slot=True):
            act.wait_ge(raw_loaded[s], 16 * (u4 + 1))
            if wait_slot:
                act.wait_ge(w_used, 4 * u4 + s - 3)
            nc.scalar.activation(w_hi[:, s, :], raw[:, s, :], ACT.Copy).then_inc(w_hi_done, 1)

        def x_high(hi, k, base, g0):
            act.wait_ge(xt_ready, base + k + 1)
            nc.scalar.activation(hi[:, k, :], x_bank(k, base)[:, :], ACT.Copy,
                                 scale=gains[:, g0 + k:g0 + k + 1]).then_inc(xt_hi_done, 1)

        def x_square(src, n, out_ap, before):
            for t in range(NT):
                if before + 4 * n + t > 0:
                    act.wait_ge(sq_done, before + 4 * n + t)
                nc.scalar.activation(out_ap, src[:, t, 512 * n:512 * (n + 1)], ACT.Square,
                                     accum_out=sums[:, t, n:n + 1]).then_inc(sq_done, 1)

        def high(dst, src, q, count, done):
            act.wait_ge(q, count)
            nc.scalar.activation(dst, src, ACT.Copy).then_inc(done, 1)

        def exps(a, h, blocks, i0):
            kind = HEAD[h][0]
            if i0 == 0 and not (isinstance(a, int) and a == 0 and h < 2):
                act.wait_ge(pt_ready, ROUNDS * a + (-2, 0, 3, 6)[h])
            for i, (b, bk, c0, _, keys, e) in enumerate(blocks):
                if kind == "A":
                    act.wait_ge(low_done, 16 * a + 4 * h + i0 + with_bank(blocks, i))
                elif i == 0:
                    act.wait_ge(sunk, 2 * a + h - 1)
                col = slice(4 * h + b, 4 * h + b + 1)
                nc.scalar.activation(probs[h % 2][:, e:e + keys], bank[bk][:, c0:c0 + keys], ACT.Exp,
                                     bias=low[:, col], scale=-1.0, accum_out=den[:, col]).then_inc(exp_done, 1)
            if kind == "B":
                nc.scalar.activation(sink_exp[:, 4 * h - 8:4 * h - 4], low[:, 4 * h:4 * h + 4], ACT.Exp,
                                     bias=sink[:, bass.ds(2 * a + h - 2, 1)], scale=1.0).then_inc(sink_done, 1)

        def pt_high(a, h, r):
            kind, _, r0 = HEAD[h]
            n = P * sum(len(q) for _, q, _ in (PT_A if kind == "A" else PT_B)[r])
            act.wait_ge(pt_ready, ROUNDS * a + r0 + r + 1)
            if not (isinstance(a, int) and a == 0 and r0 + r < 2):
                act.wait_ge(pv_done, ROUNDS * a + r0 + r - 1)
            nc.scalar.activation(pt_hi[:, (r0 + r) % 2, 0:n], bank[BANK_PT][:, 0:n], ACT.Copy).then_inc(pt_hi_done, 1)

        def o_square(a, j):
            act.wait_ge(pv_done, ROUNDS * a + (6, 10)[j])
            if not (isinstance(a, int) and a == 0 and j == 0):
                act.wait_ge(sq_added, 2 * a + j)
            nc.scalar.activation(squares[:, :], bank[BANK_O][:, :], ACT.Square).then_inc(o_sq_done, 1)

        def kv_high(kv):
            own = slice(DH * kv, DH * (kv + 1))
            if kv == 0:
                act.wait_ge(acc_taken, 1)
            else:
                act.wait_ge(s_ready, 16 * 4)
            for h in range(2):
                nc.scalar.activation(k_hi["B"][DH * h:DH * (h + 1), :], kb_all[own, :], ACT.Copy).then_inc(kb_hi_done, 1)
            if kv == 0:
                act.wait_ge(vbt_ready, 1)
                nc.scalar.activation(vb_all[:, :, :].rearrange("p t c -> p (t c)"), bank[BANK_O][:, :],
                                     ACT.Copy).then_inc(vb_all_done, 1)
                act.wait_ge(vb_all_done, 1)
                act.wait_ge(zero_done, 4)
            else:
                act.wait_ge(pv_done, ROUNDS * 4)
            for h in range(2):
                nc.scalar.activation(v_hi["B"][:, :, 3 * h, :], vb_all[:, :, own], ACT.Copy).then_inc(vb_hi_done, 1)

        def attend(s, a):
            if s == 0 and not (isinstance(a, int) and a == 0):
                o_square(a - 1, 1)
            if s == 1:
                exps(a, 0, S_A[:3], 0)
            if s == 2:
                exps(a, 0, S_A[3:], 3)
            if s == 3:
                act.wait_ge(vt_ready, a + 1)
                if isinstance(a, int) and a == 0:
                    act.wait_ge(zero_done, 4)
                nc.scalar.activation(v_hi["A"][:, :, 0:4:3, :], bank[BANK_O][:, :].rearrange("p (t h d) -> p t h d", h=2, d=DH),
                                     ACT.Copy).then_inc(va_hi_done, 1)
            if s == 4:
                exps(a, 1, S_A[:3], 0)
            if s == 5:
                exps(a, 1, S_A[3:], 3)
                pt_high(a, 0, 0)
            if s == 6:
                pt_high(a, 0, 1)
            if s == 7:
                pt_high(a, 0, 2)
                exps(a, 2, S_B, 0)
            if s in (9, 10, 11):
                pt_high(a, 1, s - 9)
            if s == 11:
                exps(a, 3, S_B, 0)
            if s == 12:
                o_square(a, 0)
                pt_high(a, 2, 0)
            if s == 13:
                pt_high(a, 2, 1)
            if s in (14, 15):
                pt_high(a, 3, s - 14)

        def pair(p, a):
            for s in range(16):
                split(*ahead(U_PAIR // 4 + 4 * p + s // 4, s % 4))
                if a is not None:
                    attend(s, a)
                if s == 1 and a is not None:
                    high(q_hi["B"][:, :], proj[1][:, :], acc_taken, 4 * p + 2, qb_hi_done)
                if s == 5:
                    if a is not None:
                        act.wait_ge(s_ready, 16 * a + 8)
                    high(q_hi["A"][:, :], proj[0][:, :], acc_taken, 4 * p + 3, qa_hi_done)
                if s == 8:
                    high(k_hi["A"][:, :], proj[1][:, :], acc_taken, 4 * p + 4, ka_hi_done)
                if s == 2 and a is None:
                    kv_high(0)

        act.dma_start(ident[:, :], c_ident).then_inc(ident_loaded, 16)
        for g, (src, r0, n) in enumerate(((attn_norm, 0, KD), (ffn_norm, KD, KD), (out_norm_a, 2 * KD, PAIRS),
                                          (out_norm_b, 2 * KD + PAIRS, PAIRS))):
            act.dma_start(gain_rows[r0:r0 + n, 0:P], src[0, :].rearrange("(k p) -> k p", p=P)).then_inc(gains_loaded, 16)
        for n in range(NC):
            act.dma_start(x_first[:, :, 512 * n:512 * (n + 1)],
                          x2[:, 512 * n:512 * (n + 1)].rearrange("(t p) c -> p t c", p=P)).then_inc(x_loaded[n], 16)
        for dst, src in ((dist, c_dist), (lnm, c_lnm), (band, c_band), (slope, c_slope), (sink, sinks[0, :].partition_broadcast(P))):
            act.dma_start(dst[:, :], src).then_inc(consts_loaded, 16)

        for u in range(4):
            split(0, u, wait_slot=False)
        act.wait_ge(gains_done, 1)
        for n in range(NC):
            for k in range(4 * n, 4 * n + 4):
                x_high(h_hi, k, 0, G_ATTN)
            if n >= 2:
                split(1, n - 2)
            act.wait_ge(x_loaded[n], 16)
            x_square(x_first, n, probs[1][:, 0:512], 0)
        for s in range(3, 8):
            split(*ahead(s // 4, s % 4))
        act.wait_ge(consts_loaded, 16 * 5)
        pair(0, None)
        pair(1, 0)
        with act.Fori(2, 5) as p:
            pair(p, p - 1)
        kv_high(1)
        with act.Fori(5, PAIRS) as p:
            pair(p, p - 1)

        def act_high(g, k):
            act.wait_ge(o_taken, (7, 15, 8, 16)[g])
            nc.scalar.activation(act_hi[:, k, :], o_t[:, 4 * g + k, :], ACT.Copy).then_inc(act_hi_done, 1)

        act.wait_ge(kb_lo_done, 4)
        act.wait_ge(vb_lo_done, 4)
        for k in range(4):
            act_high(0, k)
        for g in range(4):
            for s in range(16):
                split(*ahead(U_OUT // 4 + 4 * g + s // 4, s % 4))
                if g == 0:
                    if s == 1:
                        for n in range(NC):
                            act.dma_start(x_res[:, :, 512 * n:512 * (n + 1)],
                                          x2[:, 512 * n:512 * (n + 1)].rearrange("(t p) c -> p t c", p=P)).then_inc(x_again[n], 16)
                    attend(s, PAIRS - 1)
                    if s == 1:
                        high(q_hi["B"][:, :], proj[1][:, :], acc_taken, 4 * PAIRS + 2, qb_hi_done)
                if g == 1 and s == 0:
                    o_square(PAIRS - 1, 1)
                if s == 0 and g > 0:
                    act_high(g, 3)
                if s >= 13 and g < 3:
                    act_high(g + 1, s - 13)
                if g == 3 and s > 4 and s % 4 == 1:
                    n = s // 4 - 1
                    act.wait_ge(grp_taken, 48 + 4 * n + 4)
                    x_square(x_res, n, junk[:, :], 16)
                if g == 3 and s > 4 and s % 4 == 3:
                    for k in range(s - 7, s - 3):
                        x_high(h2_hi, k, KD, G_FFN)
        act.wait_ge(grp_taken, 64)
        x_square(x_res, 3, junk[:, :], 16)
        act.dma_start(g_fin[:, :], final_norm.partition_broadcast(P)).then_inc(gfin_loaded, 16)

        def ffn(i, first, last):
            for s in range(48):
                if not last or s < 48 - AHEAD:
                    split(*ahead(U_FFN // 4 + 12 * i + s // 4, s % 4))
                if first and s == 2:
                    for k in range(12, KD):
                        x_high(h2_hi, k, KD, G_FFN)
                if s < 32 and s % 8 == 5:
                    c = s // 8
                    act.wait_ge(gu_taken, 8 * i + 2 * c + 1)
                    if not (first and c == 0):
                        act.wait_ge(act_done, 4 * i + c)
                    nc.scalar.activation(silu_s[:, :], gate_s[:, :], ACT.Silu).then_inc(silu_done, 1)
                if s in (8, 16, 24, 32):
                    c = s // 8 - 1
                    act.wait_ge(act_done, 4 * i + c + 1)
                    nc.scalar.activation(act_hi[:, c, :], act_s[:, :], ACT.Copy).then_inc(act_hi_done, 1)
                if last and s >= 36 and s % 4 == 0:
                    n = (s - 36) // 4
                    act.wait_ge(grp_taken, 64 + 16 * (STEPS_F - 1) + 4 * n + 4)
                    x_square(x_res, n, junk[:, :], 32)

        ffn(0, True, False)
        with act.Fori(1, STEPS_F - 1) as i:
            ffn(i, False, False)
        ffn(STEPS_F - 1, False, True)
        act.wait_ge(grp_taken, 64 + 16 * STEPS_F)
        x_square(x_res, 3, junk[:, :], 32)

    @block.vector
    def _(dve):
        def split(u4, s):
            dve.wait_ge(w_hi_done, 4 * u4 + s + 1)
            nc.vector.tensor_tensor(w_lo[:, s, :], raw[:, s, :], w_hi[:, s, :].bitcast(F32), ALU.subtract).then_inc(w_lo_done, 1)

        def x_low(hi, lo, k, base, g0):
            dve.wait_ge(xt_hi_done, base + k + 1)
            nc.vector.scalar_tensor_tensor(lo[:, k, :], x_bank(k, base)[:, :], gains[:, g0 + k:g0 + k + 1],
                                           hi[:, k, :].bitcast(F32), ALU.mult, ALU.subtract).then_inc(xt_lo_done, 1)

        def low_half(dst, src, hi, q, count, done):
            dve.wait_ge(q, count)
            nc.vector.tensor_tensor(dst, src, hi.bitcast(F32), ALU.subtract).then_inc(done, 1)

        def row_means(count, n_before):
            dve.wait_ge(sq_done, 16 * count)
            nc.vector.tensor_reduce(total[:, :], sums[:, :, :], AX_X, ALU.add).then_inc(total_done, 1)
            dve.wait_ge(total_done, count)
            nc.vector.tensor_scalar(mean[:, 0:NT], total[:, :], 1.0 / D, EPS, ALU.mult, ALU.add).then_inc(mean_done, 1)

        def widen_r(wide, count, invs):
            dve.wait_ge(inv_done, invs)
            for t in range(NT):
                ins = nc.vector.tensor_scalar(wide[:, t, :], ones[:, :], inv[:, t:t + 1], None, ALU.mult)
            ins.then_inc(wide_done, 1)

        def take(dst, b, factor, used):
            dve.wait_ge(w_used, used)
            nc.vector.scalar_tensor_tensor(dst, bank[b][:, :], factor, r_bc[:, :], ALU.mult, ALU.mult).then_inc(acc_taken, 1)

        def set_bias(a, h):
            kind, odd, _ = HEAD[h]
            col = slope[:, bass.ds((0 if kind == "A" else HEADS) + 2 * a + odd, 1)]
            if kind == "A":
                nc.vector.scalar_tensor_tensor(bias[:, :], dist[:, :], col, lnm[:, :], ALU.mult, ALU.subtract).then_inc(bias_done, 1)
            else:
                nc.vector.tensor_scalar(bias[:, 0:2 * P], band[:, :], col, None, ALU.mult).then_inc(bias_done, 1)

        def lows(a, h, blocks, i0):
            kind = HEAD[h][0]
            if i0 == 0:
                dve.wait_ge(bias_done, 4 * a + h + 1)
            for i, (b, bk, c0, _, keys, _) in enumerate(blocks):
                dve.wait_ge(s_ready, 16 * a + 4 * h + i0 + with_bank(blocks, i))
                nc.vector.memset(tick[:, 4 * h + i0 + i:4 * h + i0 + i + 1], 0.0)
                s = bank[bk][:, c0:c0 + keys]
                end = SEQ if kind == "A" else 2 * P
                nc.vector.tensor_tensor_reduce(s, s, bias[:, end - keys:end], 1.0, FLOOR, ALU.add, ALU.min,
                                               low[:, 4 * h + b:4 * h + b + 1]).then_inc(low_done, 1)
            if kind == "B":
                dve.wait_ge(low_done, 16 * a + 4 * h + 4)
                four = low[:, 4 * h:4 * h + 4]
                nc.vector.tensor_scalar(four, four, neg_sink[:, bass.ds(2 * a + h - 2, 1)], None, ALU.min).then_inc(sunk, 1)

        def denominators(a, h):
            four = slice(4 * h, 4 * h + 4)
            dve.wait_ge(exp_done, 16 * a + 4 * h + 4)
            if h >= 2:
                dve.wait_ge(sink_done, 2 * a + h - 1)
                nc.vector.tensor_tensor(den[:, four], den[:, four], sink_exp[:, 4 * h - 8:4 * h - 4], ALU.add).then_inc(den_done, 1)
                dve.wait_ge(den_done, 2 * a + h - 1)
            nc.vector.reciprocal(inv_den[:, four], den[:, four]).then_inc(inv_den_done, 1)

        def pt_low(a, h, r):
            kind, _, r0 = HEAD[h]
            n = P * sum(len(q) for _, q, _ in (PT_A if kind == "A" else PT_B)[r])
            buf = (r0 + r) % 2
            low_half(pt_lo[:, buf, 0:n], bank[BANK_PT][:, 0:n], pt_hi[:, buf, 0:n], pt_hi_done, ROUNDS * a + r0 + r + 1, pt_lo_done)

        def take_o(a, j):
            dve.wait_ge(o_sq_done, 2 * a + j + 1)
            slot = PAIRS * j + a
            nc.vector.tensor_scalar(o_t[:, bass.ds(slot, 1), :].rearrange("p o c -> p (o c)"), bank[BANK_O][:, :],
                                    gains[:, bass.ds(G_OUT + slot, 1)], None, ALU.mult).then_inc(o_taken, 1)

        def kv_low(kv):
            own, other = slice(DH * kv, DH * (kv + 1)), slice(DH * (1 - kv), DH * (2 - kv))
            low_half(k_lo["B"][own, :], kb_all[own, :], k_hi["B"][own, :], kb_hi_done, 2 * kv + 2, kb_lo_done)
            dve.wait_ge(kb_lo_done, 2 * kv + 1)
            nc.vector.tensor_copy(k_lo["B"][other, :], k_lo["B"][own, :].bitcast(F32)).then_inc(kb_lo_done, 1)
            for h in range(2):
                low_half(v_lo["B"][:, :, 3 * h, :], vb_all[:, :, own], v_hi["B"][:, :, 3 * h, :], vb_hi_done, 2 * kv + h + 1, vb_lo_done)

        def attend(s, a):
            if s == 0:
                if not (isinstance(a, int) and a == 0):
                    take_o(a - 1, 1)
                set_bias(a, 0)
            if s == 1:
                lows(a, 0, S_A[:3], 0)
            if s == 2:
                lows(a, 0, S_A[3:], 3)
            if s == 3:
                denominators(a, 0)
                low_half(v_lo["A"][:, :, 0:4:3, :], bank[BANK_O][:, :].rearrange("p (t h d) -> p t h d", h=2, d=DH),
                         v_hi["A"][:, :, 0:4:3, :], va_hi_done, a + 1, va_lo_done)
                set_bias(a, 1)
            if s == 4:
                lows(a, 1, S_A[:3], 0)
            if s == 5:
                lows(a, 1, S_A[3:], 3)
                pt_low(a, 0, 0)
            if s == 6:
                denominators(a, 1)
                pt_low(a, 0, 1)
                set_bias(a, 2)
            if s == 7:
                pt_low(a, 0, 2)
                lows(a, 2, S_B, 0)
            if s == 8:
                denominators(a, 2)
            if s in (9, 10, 11):
                pt_low(a, 1, s - 9)
            if s == 9:
                set_bias(a, 3)
            if s == 10:
                lows(a, 3, S_B, 0)
            if s == 12:
                denominators(a, 3)
                take_o(a, 0)
                pt_low(a, 2, 0)
            if s == 13:
                pt_low(a, 2, 1)
            if s in (14, 15):
                pt_low(a, 3, s - 14)

        def pair(p, a):
            u = U_PAIR + 16 * p
            for s in range(16):
                split(*ahead(U_PAIR // 4 + 4 * p + s // 4, s % 4))
                if s == 0 and a is not None:
                    dve.wait_ge(ka_lo_done, p)
                    take(proj[1][:, :], BANK_K, -0.125, u)
                if s == 0 and a is None:
                    take(proj[0][:, :], BANK_K, 1.0, u)
                if a is not None:
                    attend(s, a)
                if s == 1 and a is not None:
                    low_half(q_lo["B"][:, :], proj[1][:, :], q_hi["B"][:, :], qb_hi_done, p, qb_lo_done)
                if s == 2 and a is None:
                    kv_low(0)
                if s == 4:
                    if a is None:
                        dve.wait_ge(vbt_ready, 1)
                    else:
                        dve.wait_ge(vt_ready, p)
                    take(proj[0][:, :], BANK_Q, -0.125, u + 4)
                if s == 6:
                    low_half(q_lo["A"][:, :], proj[0][:, :], q_hi["A"][:, :], qa_hi_done, p + 1, qa_lo_done)
                if s == 8:
                    take(proj[1][:, :], BANK_K, 1.0, u + 8)
                    low_half(k_lo["A"][:, :], proj[1][:, :], k_hi["A"][:, :], ka_hi_done, p + 1, ka_lo_done)
                if s == 12:
                    take(proj[0][:, :], BANK_V, 1.0, u + 12)

        dve.wait_ge(gains_turned, 1)
        rows = 2 * KD + 2 * PAIRS
        nc.vector.tensor_copy(gains[:, :], bank[BANK_Q][:, 0:rows]).then_inc(gains_done, 1)
        for u in range(4):
            split(0, u)
        dve.wait_ge(gains_done, 1)
        for n in range(NC):
            for k in range(4 * n, 4 * n + 4):
                x_low(h_hi, h_lo, k, 0, G_ATTN)
            if n >= 2:
                split(1, n - 2)
        split(1, 2)
        dve.wait_ge(ones_done, 2)
        row_means(1, 0)
        widen_r(squares[:, :].rearrange("p (t c) -> p t c", c=P), 1, 1)
        for s in range(4, 8):
            split(*ahead(1, s % 4))
            if s == 6:
                dve.wait_ge(rbc_ready, 1)
                nc.vector.tensor_copy(r_bc[:, :], bank[BANK_PT][:, :]).then_inc(rbc_done, 1)
                dve.wait_ge(rbc_done, 1)
                take(kb_all[:, :], BANK_Q, 1.0, 4)
        dve.wait_ge(consts_loaded, 16 * 5)
        nc.vector.tensor_scalar(neg_sink[:, :], sink[:, :], -1.0, None, ALU.mult).then_inc(neg_done, 1)
        dve.wait_ge(neg_done, 1)
        pair(0, None)
        pair(1, 0)
        with dve.Fori(2, 5) as p:
            pair(p, p - 1)
        kv_low(1)
        with dve.Fori(5, PAIRS) as p:
            pair(p, p - 1)

        def act_low(g, k):
            low_half(act_lo[:, k, :], o_t[:, 4 * g + k, :], act_hi[:, k, :], act_hi_done, 4 * g + k + 1, act_lo_done)

        def add_group(g, n, u4):
            cols = slice(512 * n, 512 * (n + 1))
            for t in range(NT):
                wait_group(dve, g, n, t, u4)
                b = bank[BANK_G[t]][:, :]
                xt, yt = x_res[:, t, cols], y_a[:, t, cols]
                if isinstance(g, int) and g == 0:
                    nc.vector.tensor_copy(yt, b).then_inc(grp_taken, 1)
                elif isinstance(g, int) and g == 1:
                    nc.vector.tensor_tensor(yt, b, yt, ALU.add).then_inc(grp_taken, 1)
                    if n == 0 and t == 0:
                        dve.wait_ge(inv_done, 2)
                    if t == 0:
                        dve.wait_ge(x_again[n], 16)
                    dve.wait_ge(grp_taken, 16 + 4 * n + t + 1)
                    nc.vector.scalar_tensor_tensor(xt, yt, inv[:, t:t + 1], xt, ALU.mult, ALU.add).then_inc(y_done, 1)
                elif isinstance(g, int) and g < 4:
                    nc.vector.scalar_tensor_tensor(xt, b, inv[:, 4 + t:5 + t], xt, ALU.mult, ALU.add).then_inc(grp_taken, 1)
                else:
                    nc.vector.tensor_tensor(xt, b, xt, ALU.add).then_inc(grp_taken, 1)

        for k in range(4):
            act_low(0, k)
        for g in range(4):
            u4 = U_OUT // 4 + 4 * g
            for s in range(16):
                split(*ahead(u4 + s // 4, s % 4))
                if g == 0:
                    if s == 0:
                        dve.wait_ge(ka_lo_done, PAIRS)
                        take(proj[1][:, :], BANK_K, -0.125, U_OUT)
                    attend(s, PAIRS - 1)
                    if s == 1:
                        low_half(q_lo["B"][:, :], proj[1][:, :], q_hi["B"][:, :], qb_hi_done, PAIRS, qb_lo_done)
                if g == 1 and s == 0:
                    take_o(PAIRS - 1, 1)
                if g == 1 and s == 2:
                    dve.wait_ge(ssq_ready, 1)
                    nc.vector.tensor_scalar(mean[:, :], bank[BANK_PT][:, 0:8], 1.0 / D_A, EPS, ALU.mult, ALU.add).then_inc(mean_done, 1)
                if s == 0 and g > 0:
                    act_low(g, 3)
                if s >= 13 and g < 3:
                    act_low(g + 1, s - 13)
                if g == 2 and s == 0:
                    dve.wait_ge(y_done, 16)
                if s % 4 == 3:
                    add_group(g, s // 4, u4)
                if g == 3 and s > 4 and s % 4 == 3:
                    for k in range(s - 7, s - 3):
                        x_low(h2_hi, h2_lo, k, KD, G_FFN)

        def ffn(i, first, last):
            u = U_FFN + 48 * i
            for s in range(48):
                if not last or s < 48 - AHEAD:
                    split(*ahead(U_FFN // 4 + 12 * i + s // 4, s % 4))
                if first and s == 2:
                    for k in range(12, KD):
                        x_low(h2_hi, h2_lo, k, KD, G_FFN)
                    row_means(2, 0)
                    widen_r(r2_wide, 2, 3)
                if first and s == 4:
                    dve.wait_ge(rbc_ready, 2)
                    nc.vector.tensor_copy(r2_bc[:, :], bank[BANK_X[3]][:, :]).then_inc(rbc_done, 1)
                    dve.wait_ge(rbc_done, 2)
                if s < 32 and s % 8 == 4:
                    c = s // 8
                    dve.wait_ge(w_used, u + s)
                    if not (first and c == 0):
                        dve.wait_ge(silu_done, 4 * i + c)
                    nc.vector.tensor_tensor(gate_s[:, :], bank[BANK_GATE[c % 2]][:, :], r2_bc[:, :], ALU.mult).then_inc(gu_taken, 1)
                if s in (8, 16, 24, 32):
                    c = s // 8 - 1
                    dve.wait_ge(w_used, u + s)
                    nc.vector.tensor_tensor(up_s[:, :], bank[BANK_UP[c % 2]][:, :], r2_bc[:, :], ALU.mult).then_inc(gu_taken, 1)
                    dve.wait_ge(gu_taken, 8 * i + 2 * c + 2)
                    dve.wait_ge(silu_done, 4 * i + c + 1)
                    if not (first and c == 0):
                        dve.wait_ge(act_lo_done, 16 + 4 * i + c)
                    nc.vector.tensor_tensor(act_s[:, :], up_s[:, :], silu_s[:, :], ALU.mult).then_inc(act_done, 1)
                if s in (9, 17, 25, 33):
                    c = s // 8 - 1
                    low_half(act_lo[:, c, :], act_s[:, :], act_hi[:, c, :], act_hi_done, 16 + 4 * i + c + 1, act_lo_done)
                if s >= 32 and s % 4 == 3:
                    add_group(4 + i, (s - 32) // 4, u // 4 + 8)

        ffn(0, True, False)
        with dve.Fori(1, STEPS_F - 1) as i:
            ffn(i, False, False)
        ffn(STEPS_F - 1, False, True)
        row_means(3, 0)
        dve.wait_ge(inv_done, 4)
        dve.wait_ge(gfin_loaded, 16)
        for t in range(NT):
            nc.vector.scalar_tensor_tensor(x_res[:, t, :], x_res[:, t, :], inv[:, t:t + 1], g_fin[:, :],
                                           ALU.mult, ALU.mult).then_inc(scaled, 1)

    @block.gpsimd
    def _(pool):
        def invert(count, n):
            pool.wait_ge(mean_done, count)
            nc.gpsimd.tensor_tensor(inv[:, 0:n], mean[:, 0:n], half[:, 0:n], ALU.pow).then_inc(inv_done, 1)

        def scale_rows(a, h):
            pool.wait_ge(inv_den_done, 4 * a + h + 1)
            nc.gpsimd.tensor_tensor(tick[:, 16 + h:17 + h], half[:, 0:1], half[:, 0:1], ALU.add)
            for b, _, _, _, keys, e in (S_A if HEAD[h][0] == "A" else S_B):
                row = probs[h % 2][:, e:e + keys]
                nc.gpsimd.tensor_scalar(row, row, inv_den[:, 4 * h + b:4 * h + b + 1], 1.0, ALU.mult, ALU.mult).then_inc(p_ready, 1)

        def add_squares(a, j):
            s = sq_sum["AB"[j]][:, :]
            pool.wait_ge(o_sq_done, 2 * a + j + 1)
            nc.gpsimd.tensor_tensor(s, s, squares[:, :], ALU.add).then_inc(sq_added, 1)

        def attend(a):
            if not (isinstance(a, int) and a == 0):
                add_squares(a - 1, 1)
            scale_rows(a, 0)
            scale_rows(a, 1)
            scale_rows(a, 2)
            scale_rows(a, 3)
            add_squares(a, 0)

        nc.gpsimd.memset(ones[:, :], 1.0).then_inc(ones_done, 1)
        nc.gpsimd.memset(half[:, :], -0.5).then_inc(ones_done, 1)
        for kind in "AB":
            for v in (v_hi, v_lo):
                nc.gpsimd.memset(v[kind][:, :, 1:3, :].bitcast(F32), 0.0).then_inc(zero_done, 1)
        for kind in "AB":
            nc.gpsimd.memset(sq_sum[kind][:, :], 0.0).then_inc(zero_done, 1)
        pool.wait_ge(ones_done, 2)
        pool.wait_ge(zero_done, 6)
        invert(1, NT)
        attend(0)
        with pool.Fori(1, PAIRS) as a:
            attend(a)
        add_squares(PAIRS - 1, 1)
        invert(2, 8)
        invert(3, NT)
        invert(4, NT)

    block.__exit__(None, None, None)


def constants():
    i = np.arange(P)[:, None]
    d = i + (SEQ - P) - np.arange(SEQ)[None, :]
    times = (d >= 0) * ((d <= 128) * 1 + (d % 4 == 0) + (d % 16 == 0))
    dist = np.where(times > 0, d, BIG).astype(np.float32)
    lnm = np.log(np.maximum(times, 1).astype(np.float64)).astype(np.float32)
    e = i + P - np.arange(2 * P)[None, :]
    band = np.where((e >= 0) & (e < WINDOW), e, BIG).astype(np.float32)
    idx = np.arange(2 * HEADS, dtype=np.float64)
    s = np.exp2(-8.0 * (idx + 1.0) / (2 * HEADS)).astype(np.float32)
    slope = np.tile(np.concatenate([s[0::2], s[1::2]])[None, :], (P, 1)).astype(np.float32)
    return {"c_dist": dist, "c_lnm": lnm, "c_band": band, "c_slope": np.ascontiguousarray(slope),
            "c_ident": np.eye(P, dtype=np.float32)}


INPUTS = ["x", "attn_norm", "w_in", "sinks", "out_norm_a", "out_norm_b", "w_out", "ffn_norm",
          "w_gate", "w_up", "w_down", "final_norm"]


def kernel(**inputs):
    import concourse.bacc as bacc
    from concourse.bass_utils import run_bass_kernel_spmd

    nc = bacc.Bacc("TRN2", target_bir_lowering=False, num_devices=1)
    arrays, args = {}, {}
    given = {name: np.ascontiguousarray(inputs[name]) for name in INPUTS}
    given.update(constants())
    for name, a in given.items():
        arrays[f"in_{name}"] = a
        args[name] = nc.dram_tensor(f"in_{name}", a.shape, mybir.dt.from_np(a.dtype), kind="ExternalInput").ap()
    args["out"] = nc.dram_tensor("out_x", (1, SEQ, D), F32, kind="ExternalOutput").ap()
    build(nc, **args)
    r = run_bass_kernel_spmd(nc, [arrays], core_ids=[0])
    return r.results[0]["out_x"]
```

```python
import numpy as np

import concourse.bass as bass
from concourse import mybir
from concourse.alu_op_type import AluOpType as ALU

ACT = mybir.ActivationFunctionType
AX_X = mybir.AxisListType.X
F32 = mybir.dt.float32
F32R = mybir.dt.float32r
BYTES = 4

P = 128
SEQ = 512
D = 2048
DH = 64
HEADS = 16
D_A = HEADS * DH
D_KV = 2 * DH
IN_COLS = 3 * D_A + D_A + 2 * D_KV
FF = 5632
EPS = 1e-6
NT = SEQ // P
KD = D // P
NC = D // SEQ
PAIRS = HEADS // 2
RING = 4
AHEAD = RING - 1
UNIT = 512
WINDOW = 128
BIG = 1.0e30
FLOOR = 3.0e38

U_KVB = 0
U_PAIR = 8
U_OUT = U_PAIR + 16 * PAIRS
U_FFN = U_OUT + 64
STEPS_F = FF // SEQ
UNITS = U_FFN + 48 * STEPS_F

BANK_Q, BANK_K, BANK_V = 0, 1, 4
BANK_S = (2, 3)
BANK_PT, BANK_O = 5, 7
BANK_G = (0, 4, 6, 1)
BANK_X = (2, 3, 5, 7)
BANK_GATE, BANK_UP = (2, 5), (3, 7)
START_SPLITS = ([(0, 0), (0, 1)], [(0, 2)], [(0, 3), (1, 0)], [(1, 1)])
FIRST_SQ = 4 * (NC - 1)
LAST = [(t, n) for n in range(NC) for t in (0, 1)] + [(t, n) for t in (2, 3) for n in range(NC)]
LAST_BANK = (0, 4, 6, 1, 2, 3, 5, 7)

S_A = [(3, 2, 0, 0, 512, 768), (2, 3, 0, 0, 384, 384), (0, 3, 384, 0, 128, 0), (1, 2, 0, 0, 256, 128)]
S_B = [(0, 2, 0, 0, 128, 0), (1, 2, 128, 0, 256, 128), (2, 3, 0, 128, 256, 384), (3, 3, 256, 256, 256, 640)]
E_A = {b: (e, k0) for b, _, _, k0, _, e in S_A}
E_B = {b: (e, k0) for b, _, _, k0, _, e in S_B}
PT_A = [[(0, (0, 1, 2, 3), 0)], [(1, (1, 2, 3), 0), (3, (3,), 384)], [(2, (2, 3), 0)]]
PT_B = [[(0, (0, 1), 0), (1, (1, 2), 256)], [(2, (2, 3), 0), (3, (3,), 256)]]
ROUNDS = 10
HEAD = [("A", 0, 0), ("A", 1, 3), ("B", 0, 6), ("B", 1, 8)]


def build(nc, x, attn_norm, w_in, sinks, out_norm_a, out_norm_b, w_out, ffn_norm,
          w_gate, w_up, w_down, final_norm, c_dist, c_lnm, c_band, c_slope, c_ident, out):
    spot = [(nc.sbuf_base + 63) // 64 * 64]

    def sb(name, shape, dt=F32, at=None):
        place = spot[0] if at is None else at
        size = int(np.prod(shape[1:])) * BYTES
        t = nc.alloc_sbuf_tensor_at(name, shape, dt, offset=place)
        if at is None:
            spot[0] = place + (size + 31) // 32 * 32
        assert place + size <= nc.sbuf_usable_end, name
        ends[name] = place + size
        return t

    ends = {}
    ident = sb("ident", [P, P])
    ones = sb("ones", [P, P])
    gains = sb("gains", [P, 2 * KD + 2 * PAIRS])
    sink = sb("sink", [P, HEADS])
    neg_sink = sb("neg_sink", [P, HEADS])
    slope = sb("slope", [P, 2 * HEADS])
    half = sb("half", [P, 8])
    tick = sb("tick", [P, 20])
    sums = sb("sums", [P, NT, NC])
    total = sb("total", [P, NT])
    mean = sb("mean", [P, 8])
    inv = sb("inv", [P, 8])
    raw = sb("raw", [P, RING, UNIT])
    w_hi = sb("w_hi", [P, RING, UNIT], F32R)
    w_lo = sb("w_lo", [P, RING, UNIT], F32R)
    place_x = spot[0]
    h_hi = sb("h_hi", [P, KD, SEQ], F32R)
    place_y = spot[0]
    h_lo = sb("h_lo", [P, KD, SEQ], F32R)
    place_o = spot[0]
    o_t = sb("o_t", [P, 2 * PAIRS, SEQ])
    place_g = spot[0]
    act_hi = sb("act_hi", [P, 4, SEQ], F32R)
    act_lo = sb("act_lo", [P, 4, SEQ], F32R)
    kb_all = sb("kb_all", [P, SEQ], at=place_g)
    vb_all = sb("vb_all", [P, NT, P], at=place_g + 2048)
    x_first = sb("x_first", [P, NT, D], at=place_o)
    place_att = spot[0]
    proj = [sb(f"proj{i}", [P, SEQ]) for i in range(2)]
    q_both = {g: [sb(f"q{g}_both{h}", [P, SEQ], F32R) for h in range(2)] for g in "AB"}
    k_both = {"A": [sb(f"kA_both{h}", [P, SEQ], F32R) for h in range(2)], "B": [sb("kB_both", [P, SEQ], F32R)] * 2}
    k_lo = {"A": sb("ka_lo", [P, SEQ], F32R), "B": sb("kb_lo", [P, SEQ], F32R)}
    v_both = {g: sb(f"v{g}_both", [P, NT, 4, DH], F32R) for g in "AB"}
    o_low = sb("o_low", [P, SEQ])
    dist = sb("dist", [P, SEQ])
    lnm = sb("lnm", [P, SEQ])
    band = sb("band", [P, 2 * P])
    bias = sb("bias", [P, SEQ])
    probs = [sb(f"probs{i}", [P, 10 * P]) for i in range(2)]
    pt_hi = sb("pt_hi", [P, 2, SEQ], F32R)
    pt_lo = sb("pt_lo", [P, 2, SEQ], F32R)
    squares = sb("squares", [P, SEQ])
    sq_sum = {"A": sb("sq_a", [P, SEQ]), "B": sb("sq_b", [P, SEQ])}
    r_bc = sb("r_bc", [P, SEQ])
    low = sb("low", [P, 16])
    den = sb("den", [P, 16])
    inv_den = sb("inv_den", [P, 16])
    sink_exp = sb("sink_exp", [P, 8])
    x_res = sb("x_res", [P, NT, D], at=place_x)
    y_a = sb("y_a", [P, NT, D], at=place_y)
    h2_lo = sb("h2_lo", [P, KD, SEQ], F32R, at=place_y)
    h2_hi = sb("h2_hi", [P, KD, SEQ], F32R, at=place_att)
    over = place_att + KD * SEQ * BYTES
    g_fin = sb("g_fin", [P, D], at=over)
    r2_bc = sb("r2_bc", [P, SEQ], at=over + 8192)
    r2_wide = sb("r2_wide", [P, NT, P], at=over + 10240)
    junk = sb("junk", [P, SEQ], at=over + 12288)
    gate_s = sb("gate_s", [P, SEQ], at=over + 14336)
    silu_s = sb("silu_s", [P, SEQ], at=over + 16384)
    up_s = sb("up_s", [P, SEQ], at=over + 18432)
    act_s = sb("act_s", [P, SEQ], at=over + 20480)

    bank = [nc.alloc_psum_tensor(f"bank{i}", [P, 512], F32) for i in range(8)]

    def sem(name):
        return nc.alloc_semaphore(name)

    raw_loaded = [sem(f"raw_loaded{i}") for i in range(RING)]
    w_hi_done, w_lo_done, w_used = sem("w_hi_done"), sem("w_lo_done"), sem("w_used")
    x_loaded = [sem(f"x_loaded{i}") for i in range(2 * NC)]
    x_again = [sem(f"x_again{i}") for i in range(NC)]
    consts_loaded, ident_loaded, ones_done, gains_loaded = sem("consts_loaded"), sem("ident_loaded"), sem("ones_done"), sem("gains_loaded")
    xt_ready, xt_hi_done, xt_lo_done = sem("xt_ready"), sem("xt_hi_done"), sem("xt_lo_done")
    sq_done, sq_last_done, total_done, mean_done, inv_done = sem("sq_done"), sem("sq_last_done"), sem("total_done"), sem("mean_done"), sem("inv_done")
    wide_done, rbc_ready, rbc_done = sem("wide_done"), sem("rbc_ready"), sem("rbc_done")
    acc_taken, gains_turned, gains_done = sem("acc_taken"), sem("gains_turned"), sem("gains_done")
    qa_hi_done, qa_lo_done = sem("qa_hi_done"), sem("qa_lo_done")
    ka_hi_done, ka_lo_done = sem("ka_hi_done"), sem("ka_lo_done")
    qb_hi_done, qb_lo_done = sem("qb_hi_done"), sem("qb_lo_done")
    kb_hi_done, kb_lo_done = sem("kb_hi_done"), sem("kb_lo_done")
    vt_ready, va_hi_done, va_lo_done = sem("vt_ready"), sem("va_hi_done"), sem("va_lo_done")
    vbt_ready, vb_all_done = sem("vbt_ready"), sem("vb_all_done")
    vb_hi_done, vb_lo_done, zero_done = sem("vb_hi_done"), sem("vb_lo_done"), sem("zero_done")
    s_ready, bias_done, low_done, sunk = sem("s_ready"), sem("bias_done"), sem("low_done"), sem("sunk")
    exp_done, sink_done, den_done, inv_den_done = sem("exp_done"), sem("sink_done"), sem("den_done"), sem("inv_den_done")
    p_ready, pt_ready, pt_hi_done, pt_lo_done = sem("p_ready"), sem("pt_ready"), sem("pt_hi_done"), sem("pt_lo_done")
    pv_done, o_low_done, o_sq_done, o_taken, sq_added = sem("pv_done"), sem("o_low_done"), sem("o_sq_done"), sem("o_taken"), sem("sq_added")
    ssq_ready, act_hi_done, act_lo_done = sem("ssq_ready"), sem("act_hi_done"), sem("act_lo_done")
    grp_ready, grp_taken, y_done = sem("grp_ready"), sem("grp_taken"), sem("y_done")
    gu_ready, gu_taken, silu_done, act_done = sem("gu_ready"), sem("gu_taken"), sem("silu_done"), sem("act_done")
    neg_done, gfin_loaded = sem("neg_done"), sem("gfin_loaded")
    scaled, stored = sem("scaled"), sem("stored")
    last_ready, gained, scaled_act = sem("last_ready"), sem("gained"), sem("scaled_act")

    w_in2, w_out2 = w_in[0], w_out[0]
    w_gate2, w_up2, w_down2 = w_gate[0], w_up[0], w_down[0]
    x2, out2 = x[0], out[0]
    gain_rows = probs[0]
    G_ATTN, G_FFN, G_OUT = 0, KD, 2 * KD

    block = nc.Block()
    block.__enter__()

    def col_in(kind, p):
        return {"q": 0, "k": D_A, "v": 2 * D_A, "qb": 3 * D_A}[kind] + p * P

    def ahead(v4, s):
        return (v4, AHEAD) if s == 0 else (v4 + 1, s - 1)

    def x_bank(k, base):
        return bank[(BANK_G if base and k >= KD - 4 else BANK_X)[k % 4]]

    def group_bank(n, t, ffn):
        return bank[(BANK_X if ffn and n % 2 else BANK_G)[t]]

    def last_weights(n, k):
        if n == 0:
            return w_hi[:, k, :], w_lo[:, k, :]
        return h2_hi[:, 4 * n + k, :], h2_lo[:, 4 * n + k, :]

    def with_bank(blocks, i):
        return max(j for j, b in enumerate(blocks) if b[1] == blocks[i][1]) + 1

    def wait_group(eng, g, n, t, u4):
        if t < NT - 1:
            eng.wait_ge(grp_ready, 3 * (4 * g + n) + t + 1)
        else:
            eng.wait_ge(w_used, 4 * (u4 + n) + 4)

    @block.sync
    def _(sp):
        def load(u4, s, src, first=False):
            if not first:
                sp.wait_ge(w_lo_done, 4 * u4 - 3 + s)
            dst = raw[:, s, :]
            if len(src.shape) == 3:
                dst = dst.rearrange("p (k c) -> p k c", c=P)
            sp.dma_start(dst, src).then_inc(raw_loaded[s], 16)

        def tall(w, j, col):
            return w[512 * j:512 * (j + 1), bass.ds(col, P)].rearrange("(k p) c -> p k c", p=P)

        sp.dma_start(ident[:, :], c_ident).then_inc(ident_loaded, 16)
        for n in range(2 * NC):
            cols = slice(256 * n, 256 * (n + 1))
            sp.dma_start(x_first[:, :, cols], x2[:, cols].rearrange("(t p) c -> p t c", p=P)).then_inc(x_loaded[n], 16)
            if n % 2:
                load(0, n // 2, tall(w_in2, n // 2, 4 * D_A), first=True)
        for j in range(4):
            load(1, j, tall(w_in2, j, 4 * D_A + D_KV))
        with sp.Fori(0, PAIRS) as p:
            for c, kind in enumerate(("q", "k", "v", "qb")):
                for j in range(4):
                    load(U_PAIR // 4 + 4 * p + c, j, tall(w_in2, j, col_in(kind, p)))
        with sp.Fori(0, 4) as g:
            for n in range(NC):
                for k in range(4):
                    load(U_OUT // 4 + 4 * g + n, k, w_out2[bass.ds(g * 512 + P * k, P), 512 * n:512 * (n + 1)])
        with sp.Fori(0, STEPS_F) as i:
            for c in range(4):
                for h, w in enumerate((w_gate2, w_up2)):
                    for j in range(4):
                        load(U_FFN // 4 + 12 * i + 2 * c + h, j, tall(w, j, i * 512 + P * c))
            for n in range(NC):
                for k in range(4):
                    load(U_FFN // 4 + 12 * i + 8 + n, k,
                         w_down2[bass.ds(i * 512 + P * k, P), 512 * n:512 * (n + 1)])
        for t in range(NT - 1):
            sp.wait_ge(scaled, t + 1)
            sp.dma_start(out2[P * t:P * (t + 1), :], x_res[:, t, :]).then_inc(stored, 16)
        sp.wait_ge(scaled, NT)
        sp.dma_start(out2[P * (NT - 1):SEQ, 0:D // 2], x_res[:, NT - 1, 0:D // 2]).then_inc(stored, 16)
        sp.wait_ge(stored, 16 * (NT + 1))

    @block.tensor
    def _(pe):
        def three(out_ap, st_hi, st_lo, mv_hi, mv_lo, start, stop):
            nc.tensor.matmul(out_ap, st_hi, mv_hi, start=start, stop=False, skip_group_check=True)
            nc.tensor.matmul(out_ap, st_hi, mv_lo, start=False, stop=False, skip_group_check=True)
            return nc.tensor.matmul(out_ap, st_lo, mv_hi, start=False, stop=stop, skip_group_check=True)

        def turn_x(src, k, base):
            if base + k >= 4:
                pe.wait_ge(xt_lo_done, base + k - 3)
            b = x_bank(k, base)
            for t in range(NT):
                mm = nc.tensor.transpose(b[:, P * t:P * (t + 1)], src[:, t, P * k:P * (k + 1)], ident[:, :])
            mm.then_inc(xt_ready, 1)

        def spread_r(wide, count, b):
            pe.wait_ge(wide_done, count)
            for t in range(NT):
                mm = nc.tensor.matmul(bank[b][:, P * t:P * (t + 1)], wide[:, t, :], ident[:, :], start=True, stop=True)
            mm.then_inc(rbc_ready, 1)

        def tall_unit(u4, j, b, hh, hl):
            pe.wait_ge(w_lo_done, 4 * u4 + j + 1)
            for k in range(4):
                ws = slice(P * k, P * (k + 1))
                mm = three(bank[b][:, :], w_hi[:, j, ws], w_lo[:, j, ws], hh[:, 4 * j + k, :], hl[:, 4 * j + k, :],
                           j == 0 and k == 0, j == 3 and k == 3)
            mm.then_inc(w_used, 1)

        def wide_unit(u4, s, g, split, ffn=False):
            n, k = s // 4, s % 4
            pe.wait_ge(w_lo_done, 4 * (u4 + n) + k + 1)
            if n == 0:
                pe.wait_ge(act_lo_done, split + k + 1)
            for t in range(NT):
                ts, b = slice(P * t, P * (t + 1)), group_bank(n, t, ffn)
                if k == 0 and ffn:
                    if n == 1 and t == 0:
                        pe.wait_ge(gu_taken, 8 * (g - 3))
                    if n != 1:
                        pe.wait_ge(grp_taken, 16 * g + 4 * n + t - 7)
                elif k == 0 and not (isinstance(g, int) and g == 0 and n == 0):
                    pe.wait_ge(grp_taken, 16 * g + 4 * n + t - 3)
                if k == 0 and isinstance(g, int) and g == 0 and n == 0:
                    pe.wait_ge(acc_taken, 2 + 4 * PAIRS if BANK_G[t] == BANK_K else 1 + 4 * PAIRS)
                nc.tensor.matmul(b[:, :], act_hi[:, k, ts], w_hi[:, k, :], start=k == 0, stop=False, skip_group_check=True)
                nc.tensor.matmul(b[:, :], act_hi[:, k, ts], w_lo[:, k, :], start=False, stop=False, skip_group_check=True)
                mm = nc.tensor.matmul(b[:, :], act_lo[:, k, ts], w_hi[:, k, :], start=False, stop=k == 3, skip_group_check=True)
                if k == 3 and t < NT - 1:
                    mm.then_inc(grp_ready, 1)
            mm.then_inc(w_used, 1)

        def scores(a, h, blocks):
            kind, odd, _ = HEAD[h]
            rows = slice(DH * odd, DH * (odd + 1))
            q, kh, kl = q_both[kind][odd], k_both[kind][odd], k_lo[kind]
            for b, bk, c0, k0, keys, _ in blocks:
                qs, ks, s = slice(P * b, P * (b + 1)), slice(k0, k0 + keys), bank[bk][:, c0:c0 + keys]
                nc.tensor.matmul(s, q[:, qs], kh[:, ks], start=True, stop=False, skip_group_check=True)
                nc.tensor.matmul(s, q[rows, qs], kl[rows, ks], start=False, stop=True,
                                 skip_group_check=True).then_inc(s_ready, 1)

        def turn_p(a, h, r):
            kind, _, r0 = HEAD[h]
            if r == 0:
                pe.wait_ge(p_ready, 16 * a + 4 * (h + 1))
            if not (isinstance(a, int) and a == 0 and r0 + r == 0):
                pe.wait_ge(pt_lo_done, ROUNDS * a + r0 + r)
            where = E_A if kind == "A" else E_B
            for kb, qbs, c0 in (PT_A if kind == "A" else PT_B)[r]:
                for n, qb in enumerate(qbs):
                    e, k0 = where[qb]
                    e += P * kb - k0
                    mm = nc.tensor.transpose(bank[BANK_PT][:, c0 + P * n:c0 + P * (n + 1)],
                                             probs[h % 2][:, e:e + P], ident[:, :])
            mm.then_inc(pt_ready, 1)

        def weigh_v(a, h, r):
            kind, odd, r0 = HEAD[h]
            rounds = PT_A if kind == "A" else PT_B
            pe.wait_ge(pt_lo_done, ROUNDS * a + r0 + r + 1)
            if r == 0 and h > 0:
                pe.wait_ge(o_taken, 4 * a + h)
            buf = (r0 + r) % 2
            for i, (kb, qbs, c0) in enumerate(rounds[r]):
                n = P * len(qbs)
                v = v_both[kind][:, kb, 2 * odd:2 * odd + 2, :].rearrange("p a d -> p (a d)")
                o = bank[BANK_O][:, P * qbs[0]:P * qbs[0] + n]
                nc.tensor.matmul(o, v, pt_hi[:, buf, c0:c0 + n], start=r == 0 and i == 0, stop=False, skip_group_check=True)
                mm = nc.tensor.matmul(o, v, pt_lo[:, buf, c0:c0 + n], start=False,
                                      stop=r == len(rounds) - 1 and i == len(rounds[r]) - 1, skip_group_check=True)
            mm.then_inc(pv_done, 1)

        def turn_v():
            for t in range(NT):
                mm = nc.tensor.transpose(bank[BANK_O][:, P * t:P * (t + 1)], proj[0][:, P * t:P * (t + 1)], ident[:, :])
            return mm

        def attend(s, a, kv):
            first = isinstance(a, int) and a == 0
            if s == 0:
                pe.wait_ge(qa_lo_done, 2 * (a + 1))
                pe.wait_ge(ka_lo_done, 2 * (a + 1))
                pe.wait_ge(ka_hi_done, 4 * (a + 1))
                if not first:
                    pe.wait_ge(exp_done, 16 * a)
                scores(a, 0, S_A[:3])
            if s == 1:
                pe.wait_ge(exp_done, 16 * a + 1)
                scores(a, 0, S_A[3:])
            if s == 2:
                pe.wait_ge(acc_taken, 5 + 4 * a)
                if first:
                    pe.wait_ge(vb_all_done, 1)
                else:
                    pe.wait_ge(o_taken, 4 * a)
                turn_v().then_inc(vt_ready, 1)
            if s == 3:
                pe.wait_ge(exp_done, 16 * a + 4)
                scores(a, 1, S_A[:3])
            if s == 4:
                turn_p(a, 0, 0)
                pe.wait_ge(exp_done, 16 * a + 5)
                scores(a, 1, S_A[3:])
            if s == 5:
                turn_p(a, 0, 1)
                pe.wait_ge(va_lo_done, a + 1)
                weigh_v(a, 0, 0)
            if s == 6:
                turn_p(a, 0, 2)
                weigh_v(a, 0, 1)
                pe.wait_ge(qb_lo_done, 2 * (a + 1))
                pe.wait_ge(kb_lo_done, 2 * (kv + 1))
                pe.wait_ge(exp_done, 16 * a + 8)
                scores(a, 2, S_B)
            if s == 7:
                weigh_v(a, 0, 2)
            if s == 8:
                turn_p(a, 1, 0)
            if s == 9:
                turn_p(a, 1, 1)
                weigh_v(a, 1, 0)
                pe.wait_ge(exp_done, 16 * a + 12)
                scores(a, 3, S_B)
            if s == 10:
                turn_p(a, 1, 2)
                weigh_v(a, 1, 1)
            if s == 11:
                weigh_v(a, 1, 2)
                turn_p(a, 2, 0)
            if s == 12:
                turn_p(a, 2, 1)
            if s == 13:
                pe.wait_ge(vb_lo_done, 2 * (kv + 1))
                weigh_v(a, 2, 0)
                turn_p(a, 3, 0)
            if s == 14:
                weigh_v(a, 2, 1)
                turn_p(a, 3, 1)
            if s == 15:
                weigh_v(a, 3, 0)
                weigh_v(a, 3, 1)

        def pair(p, a, kv):
            for c, b in enumerate((BANK_Q, BANK_K, BANK_V, BANK_K)):
                if c == 0:
                    pe.wait_ge(acc_taken, 1 if a is None else 4 * p - 1)
                if c in (1, 3):
                    pe.wait_ge(acc_taken, 4 * p + c + 1)
                if c == 2 and a is not None:
                    pe.wait_ge(acc_taken, 4 * p + 1)
                for j in range(4):
                    tall_unit(U_PAIR // 4 + 4 * p + c, j, b, h_hi, h_lo)
                    if a is not None:
                        attend(4 * c + j, a, kv)
                    if a is None and c == 0 and j == 1:
                        pe.wait_ge(acc_taken, 2)
                        turn_v().then_inc(vbt_ready, 1)
                    if a is None and c == 3 and j == 2:
                        pe.wait_ge(gains_loaded, 16 * 4)
                        n = KD + 2 * PAIRS
                        nc.tensor.transpose(bank[BANK_PT][:, 0:n], gain_rows[0:n, P:2 * P], ident[0:n, 0:n]).then_inc(gains_turned, 1)

        pe.wait_ge(ident_loaded, 16)
        for k in range(8):
            if k % 2 == 0:
                pe.wait_ge(x_loaded[k // 2], 16)
            turn_x(x_first, k, 0)
            if k == 1:
                pe.wait_ge(gains_loaded, 16)
                nc.tensor.transpose(bank[BANK_Q][:, 0:KD], gain_rows[0:KD, 0:P],
                                    ident[0:KD, 0:KD]).then_inc(gains_turned, 1)
        pe.wait_ge(gains_done, 1)
        for s in range(8):
            if s < 4:
                pe.wait_ge(xt_lo_done, 4 * s + 4)
            tall_unit(s // 4, s % 4, (BANK_Q, BANK_K)[s // 4], h_hi, h_lo)
            if s < 2:
                for k in range(8 + 4 * s, 12 + 4 * s):
                    if k % 2 == 0:
                        pe.wait_ge(x_loaded[k // 2], 16)
                    turn_x(x_first, k, 0)
            if s == 6:
                pe.wait_ge(xt_lo_done, KD)
                spread_r(squares[:, :].rearrange("p (t c) -> p t c", c=P), 1, BANK_PT)
        pe.wait_ge(rbc_done, 1)
        pair(0, None, 0)
        pe.wait_ge(gains_done, 2)
        pair(1, 0, 0)
        with pe.Fori(2, 5) as p:
            pair(p, p - 1, 0)
        with pe.Fori(5, PAIRS) as p:
            pair(p, p - 1, 1)

        for g in range(4):
            for s in range(16):
                wide_unit(U_OUT // 4 + 4 * g, s, g, 4 * g)
                if g == 0:
                    attend(s, PAIRS - 1, 1)
                if g == 1 and s == 2:
                    pe.wait_ge(sq_added, 2 * PAIRS)
                    pe.wait_ge(pt_lo_done, ROUNDS * PAIRS)
                    for i, kind in enumerate("AB"):
                        for t in range(NT):
                            mm = nc.tensor.matmul(bank[BANK_PT][:, 4 * i + t:4 * i + t + 1],
                                                  sq_sum[kind][:, P * t:P * (t + 1)], ones[:, 0:1], start=True, stop=True)
                    mm.then_inc(ssq_ready, 1)
                if g == 3 and s % 4 == 2 and s > 4:
                    n = s // 4 - 1
                    pe.wait_ge(grp_taken, 16 * g + 4 * n + 4)
                    for k in range(4 * n, 4 * n + 4):
                        turn_x(x_res, k, KD)

        def ffn(i, first, last=False):
            u = U_FFN // 4 + 12 * i
            for c in range(4):
                for h, banks in enumerate((BANK_GATE, BANK_UP)):
                    b = banks[c % 2]
                    if c >= 2:
                        pe.wait_ge(gu_taken, 8 * i + 2 * c + h - 3)
                    elif not first:
                        pe.wait_ge(grp_taken, 16 * (4 + i) - 3 + BANK_X.index(b))
                    elif b != BANK_X[3]:
                        pe.wait_ge(xt_lo_done, 2 * KD - 8 + BANK_X.index(b) + 1)
                    else:
                        pe.wait_ge(rbc_done, 2)
                    for j in range(4):
                        if first and c == 0 and h == 0:
                            pe.wait_ge(xt_lo_done, KD + 4 * j + 4)
                        tall_unit(u + 2 * c + h, j, b, h2_hi, h2_lo)
                        if first and c == 0 and h == 0 and j == 1:
                            pe.wait_ge(grp_taken, 64)
                            for k in range(12, KD):
                                turn_x(x_res, k, KD)
                        if first and c == 0 and h == 0 and j == 3:
                            pe.wait_ge(xt_lo_done, 2 * KD)
                            spread_r(r2_wide, 2, BANK_X[3])
            if not last:
                for s in range(16):
                    wide_unit(u + 8, s, 4 + i, 16 + 4 * i, ffn=True)

        def last_products(g, u):
            for m, (t, n) in enumerate(LAST):
                if m % 2 and m < 8:
                    continue
                todo = [(m, t), (m + 1, t + 1)] if m < 8 else [(m, t)]
                for k in range(4):
                    if m < 8:
                        pe.wait_ge(w_lo_done, 4 * (u + 8 + n) + k + 1)
                    if m == 0:
                        pe.wait_ge(act_lo_done, 4 * g + k + 1)
                    for mi, ti in todo:
                        if k == 0 and mi < 8:
                            pe.wait_ge(grp_taken, 16 * g - 7 + BANK_G.index(LAST_BANK[mi]) if mi < 4 else 16 * g)
                            if mi == 4:
                                pe.wait_ge(gu_taken, 8 * STEPS_F)
                        elif k == 0:
                            pe.wait_ge(grp_taken, 16 * g + mi - 7)
                        b, ts = bank[LAST_BANK[mi % 8]], slice(P * ti, P * (ti + 1))
                        wh, wl = last_weights(n, k)
                        mm = three(b[:, :], act_hi[:, k, ts], act_lo[:, k, ts], wh, wl, k == 0, k == 3)
                        if k == 3:
                            mm.then_inc(last_ready, 1)

        ffn(0, True)
        with pe.Fori(1, STEPS_F - 1) as i:
            ffn(i, False)
        ffn(STEPS_F - 1, False, last=True)
        last_products(3 + STEPS_F, U_FFN // 4 + 12 * (STEPS_F - 1))

    @block.scalar
    def _(act):
        def split(u4, s, wait_slot=True):
            act.wait_ge(raw_loaded[s], 16 * (u4 + 1))
            if wait_slot:
                act.wait_ge(w_used, 4 * u4 + s - 3)
            nc.scalar.activation(w_hi[:, s, :], raw[:, s, :], ACT.Copy).then_inc(w_hi_done, 1)

        def x_high(hi, k, base, g0):
            act.wait_ge(xt_ready, base + k + 1)
            nc.scalar.activation(hi[:, k, :], x_bank(k, base)[:, :], ACT.Copy,
                                 scale=gains[:, g0 + k:g0 + k + 1]).then_inc(xt_hi_done, 1)

        def x_square(src, n, out_ap, before):
            for t in range(NT):
                if before + 4 * n + t > 0:
                    act.wait_ge(sq_done, before + 4 * n + t)
                nc.scalar.activation(out_ap, src[:, t, 512 * n:512 * (n + 1)], ACT.Square,
                                     accum_out=sums[:, t, n:n + 1]).then_inc(sq_done, 1)

        def q_high(kind, src, count, done):
            act.wait_ge(acc_taken, count)
            for h in range(2):
                own = slice(DH * h, DH * (h + 1))
                nc.scalar.activation(q_both[kind][h][own, :], src[own, :], ACT.Copy).then_inc(done, 1)

        def k_high(count, swap):
            act.wait_ge(acc_taken, count)
            for h in range(2):
                own, to = slice(DH * h, DH * (h + 1)), 1 - h if swap else h
                nc.scalar.activation(k_both["A"][h][DH * to:DH * (to + 1), :], proj[1][own, :],
                                     ACT.Copy).then_inc(ka_hi_done, 1)

        def exps(a, h, blocks, i0):
            kind = HEAD[h][0]
            if i0 == 0 and not (isinstance(a, int) and a == 0 and h < 2):
                act.wait_ge(pt_ready, ROUNDS * a + (-2, 0, 3, 6)[h])
            for i, (b, bk, c0, _, keys, e) in enumerate(blocks):
                if kind == "A":
                    act.wait_ge(low_done, 16 * a + 4 * h + i0 + with_bank(blocks, i))
                elif i == 0:
                    act.wait_ge(sunk, 2 * a + h - 1)
                col = slice(4 * h + b, 4 * h + b + 1)
                nc.scalar.activation(probs[h % 2][:, e:e + keys], bank[bk][:, c0:c0 + keys], ACT.Exp,
                                     bias=low[:, col], scale=-1.0, accum_out=den[:, col]).then_inc(exp_done, 1)
            if kind == "B":
                nc.scalar.activation(sink_exp[:, 4 * h - 8:4 * h - 4], low[:, 4 * h:4 * h + 4], ACT.Exp,
                                     bias=sink[:, bass.ds(2 * a + h - 2, 1)], scale=1.0).then_inc(sink_done, 1)

        def pt_high(a, h, r):
            kind, _, r0 = HEAD[h]
            n = P * sum(len(q) for _, q, _ in (PT_A if kind == "A" else PT_B)[r])
            act.wait_ge(pt_ready, ROUNDS * a + r0 + r + 1)
            if not (isinstance(a, int) and a == 0 and r0 + r < 2):
                act.wait_ge(pv_done, ROUNDS * a + r0 + r - 1)
            nc.scalar.activation(pt_hi[:, (r0 + r) % 2, 0:n], bank[BANK_PT][:, 0:n], ACT.Copy).then_inc(pt_hi_done, 1)

        def o_lower(a, h):
            odd = HEAD[h][1]
            own, other = slice(DH * odd, DH * (odd + 1)), slice(DH * (1 - odd), DH * (2 - odd))
            act.wait_ge(pv_done, ROUNDS * a + (3, 6, 8, 10)[h])
            if not (isinstance(a, int) and a == 0 and h < 2):
                act.wait_ge(o_taken, 4 * a + h - 1)
            nc.scalar.activation(o_low[own, :], bank[BANK_O][other, :], ACT.Copy).then_inc(o_low_done, 1)

        def o_square(a, j):
            act.wait_ge(o_taken, 4 * a + 2 * j + 2)
            if not (isinstance(a, int) and a == 0 and j == 0):
                act.wait_ge(sq_added, 2 * a + j)
            nc.scalar.activation(squares[:, :], o_t[:, bass.ds(PAIRS * j + a, 1), :].rearrange("p o c -> p (o c)"),
                                 ACT.Square).then_inc(o_sq_done, 1)

        def kv_high(kv):
            own = slice(DH * kv, DH * (kv + 1))
            if kv == 0:
                act.wait_ge(acc_taken, 1)
            else:
                act.wait_ge(s_ready, 16 * 4)
            for h in range(2):
                nc.scalar.activation(k_both["B"][0][DH * h:DH * (h + 1), :], kb_all[own, :], ACT.Copy).then_inc(kb_hi_done, 1)
            if kv == 0:
                act.wait_ge(vbt_ready, 1)
                nc.scalar.activation(vb_all[:, :, :].rearrange("p t c -> p (t c)"), bank[BANK_O][:, :],
                                     ACT.Copy).then_inc(vb_all_done, 1)
                act.wait_ge(vb_all_done, 1)
            else:
                act.wait_ge(pv_done, ROUNDS * 4)
            for h in range(2):
                nc.scalar.activation(v_both["B"][:, :, 3 * h, :], vb_all[:, :, own], ACT.Copy).then_inc(vb_hi_done, 1)

        def attend(s, a):
            if s == 0 and not (isinstance(a, int) and a == 0):
                o_lower(a - 1, 3)
            if s == 1 and not (isinstance(a, int) and a == 0):
                o_square(a - 1, 1)
            if s == 1:
                exps(a, 0, S_A[:3], 0)
            if s == 2:
                exps(a, 0, S_A[3:], 3)
            if s == 3:
                act.wait_ge(vt_ready, a + 1)
                nc.scalar.activation(v_both["A"][:, :, 0:4:3, :], bank[BANK_O][:, :].rearrange("p (t h d) -> p t h d", h=2, d=DH),
                                     ACT.Copy).then_inc(va_hi_done, 1)
            if s == 4:
                exps(a, 1, S_A[:3], 0)
            if s == 5:
                pt_high(a, 0, 0)
                exps(a, 1, S_A[3:], 3)
            if s == 6:
                pt_high(a, 0, 1)
            if s == 7:
                pt_high(a, 0, 2)
                exps(a, 2, S_B, 0)
            if s == 8:
                o_lower(a, 0)
            if s in (9, 10, 11):
                pt_high(a, 1, s - 9)
            if s == 11:
                exps(a, 3, S_B, 0)
            if s == 12:
                o_lower(a, 1)
                pt_high(a, 2, 0)
            if s == 13:
                o_square(a, 0)
                pt_high(a, 2, 1)
            if s == 15:
                o_lower(a, 2)
            if s in (14, 15):
                pt_high(a, 3, s - 14)

        def pair(p, a):
            for s in range(16):
                split(*ahead(U_PAIR // 4 + 4 * p + s // 4, s % 4))
                if a is not None:
                    attend(s, a)
                if s == 1 and a is not None:
                    q_high("B", proj[1], 4 * p + 2, qb_hi_done)
                if s == 5:
                    if a is not None:
                        act.wait_ge(s_ready, 16 * a + 8)
                    q_high("A", proj[0], 4 * p + 3, qa_hi_done)
                if s in (9, 10):
                    k_high(4 * p + 4, s == 10)
                if s == 2 and a is None:
                    kv_high(0)

        act.dma_start(gain_rows[0:KD, 0:P], attn_norm[0, :].rearrange("(k p) -> k p", p=P)).then_inc(gains_loaded, 16)

        act.wait_ge(gains_done, 1)
        for n in range(NC):
            for k in range(4 * n, 4 * n + 4):
                x_high(h_hi, k, 0, G_ATTN)
            for u4, slot in START_SPLITS[n]:
                split(u4, slot, wait_slot=u4 > 0)
            act.wait_ge(x_loaded[2 * n], 16)
            act.wait_ge(x_loaded[2 * n + 1], 16)
            for m in ((), (0,), (), (1,))[n]:
                x_square(x_first, m, probs[1][:, 0:512], 0)
        for dst, src in ((dist, c_dist), (lnm, c_lnm), (band, c_band), (slope, c_slope), (sink, sinks[0, :].partition_broadcast(P))):
            act.dma_start(dst[:, :], src).then_inc(consts_loaded, 16)
        for src, r0, n in ((ffn_norm, 0, KD), (out_norm_a, KD, PAIRS), (out_norm_b, KD + PAIRS, PAIRS)):
            act.dma_start(gain_rows[r0:r0 + n, P:2 * P], src[0, :].rearrange("(k p) -> k p", p=P)).then_inc(gains_loaded, 16)
        for s in range(3, 8):
            split(*ahead(s // 4, s % 4))
            if s == 3:
                x_square(x_first, 2, probs[1][:, 0:512], 0)
        act.wait_ge(consts_loaded, 16 * 5)
        pair(0, None)
        pair(1, 0)
        with act.Fori(2, 5) as p:
            pair(p, p - 1)
        kv_high(1)
        with act.Fori(5, PAIRS) as p:
            pair(p, p - 1)

        def act_high(g, k):
            act.wait_ge(o_taken, (14, 30, 16, 32)[g])
            nc.scalar.activation(act_hi[:, k, :], o_t[:, 4 * g + k, :], ACT.Copy,
                                 scale=gains[:, G_OUT + 4 * g + k:G_OUT + 4 * g + k + 1]).then_inc(act_hi_done, 1)

        act.wait_ge(kb_lo_done, 4)
        act.wait_ge(vb_lo_done, 4)
        for k in range(4):
            act_high(0, k)
        for g in range(4):
            for s in range(16):
                split(*ahead(U_OUT // 4 + 4 * g + s // 4, s % 4))
                if g == 0:
                    if s == 1:
                        for n in range(NC):
                            act.dma_start(x_res[:, :, 512 * n:512 * (n + 1)],
                                          x2[:, 512 * n:512 * (n + 1)].rearrange("(t p) c -> p t c", p=P)).then_inc(x_again[n], 16)
                    attend(s, PAIRS - 1)
                    if s == 1:
                        q_high("B", proj[1], 4 * PAIRS + 2, qb_hi_done)
                if g == 1 and s == 0:
                    o_lower(PAIRS - 1, 3)
                    o_square(PAIRS - 1, 1)
                if s == 0 and g > 0:
                    act_high(g, 3)
                if s >= 13 and g < 3:
                    act_high(g + 1, s - 13)
                if g == 3 and s > 4 and s % 4 == 1:
                    n = s // 4 - 1
                    act.wait_ge(grp_taken, 48 + 4 * n + 4)
                    x_square(x_res, n, junk[:, :], FIRST_SQ)
                if g == 3 and s > 4 and s % 4 == 3:
                    for k in range(s - 7, s - 3):
                        x_high(h2_hi, k, KD, G_FFN)
        act.wait_ge(grp_taken, 64)
        x_square(x_res, 3, junk[:, :], FIRST_SQ)
        act.dma_start(g_fin[:, :], final_norm.partition_broadcast(P)).then_inc(gfin_loaded, 16)

        def squares_of(m0, count):
            for m in range(m0, m0 + count):
                t, n = LAST[m]
                act.wait_ge(grp_taken, 16 * (3 + STEPS_F) + m + 1)
                act.wait_ge(sq_done, FIRST_SQ + 16 + m)
                nc.scalar.activation(junk[:, :], x_res[:, t, 512 * n:512 * (n + 1)], ACT.Square,
                                     accum_out=sums[:, t, n:n + 1]).then_inc(sq_done, 1)

        def ffn(i, first, last):
            for s in range(32 if last else 48):
                split(*ahead(U_FFN // 4 + 12 * i + s // 4, s % 4))
                if first and s == 2:
                    for k in range(12, KD):
                        x_high(h2_hi, k, KD, G_FFN)
                if s < 32 and s % 8 == 5:
                    c = s // 8
                    act.wait_ge(gu_taken, 8 * i + 2 * c + 1)
                    if not (first and c == 0):
                        act.wait_ge(act_done, 4 * i + c)
                    nc.scalar.activation(silu_s[:, :], gate_s[:, :], ACT.Silu).then_inc(silu_done, 1)
                if s in (8, 16, 24, 32):
                    c = s // 8 - 1
                    act.wait_ge(act_done, 4 * i + c + 1)
                    nc.scalar.activation(act_hi[:, c, :], act_s[:, :], ACT.Copy).then_inc(act_hi_done, 1)

        ffn(0, True, False)
        with act.Fori(1, STEPS_F - 1) as i:
            ffn(i, False, False)
        ffn(STEPS_F - 1, False, True)
        u4 = U_FFN // 4 + 12 * STEPS_F - 4
        split(u4, AHEAD)
        act.wait_ge(act_done, 4 * STEPS_F)
        nc.scalar.activation(act_hi[:, 3, :], act_s[:, :], ACT.Copy).then_inc(act_hi_done, 1)
        act.wait_ge(w_used, 4 * u4)
        done = 0
        for j in range(4, 16):
            act.wait_ge(raw_loaded[j % 4], 16 * (u4 + j // 4 + 1))
            nc.scalar.activation(h2_hi[:, j, :], raw[:, j % 4, :], ACT.Copy).then_inc(w_hi_done, 1)
            if j in (9, 13):
                squares_of(done, 2)
                done += 2
        squares_of(done, 16 - done)
        act.wait_ge(inv_done, 7)
        act.wait_ge(gained, NC)
        nc.scalar.activation(x_res[:, NT - 1, D // 2:D], o_t[:, 2:4, :].rearrange("p a c -> p (a c)"), ACT.Copy,
                             scale=inv[:, NT - 1:NT]).then_inc(scaled_act, 1)
        act.wait_ge(scaled_act, 1)
        act.dma_start(out2[P * (NT - 1):SEQ, D // 2:D], x_res[:, NT - 1, D // 2:D]).then_inc(stored, 16)

    @block.vector
    def _(dve):
        def split(u4, s):
            dve.wait_ge(w_hi_done, 4 * u4 + s + 1)
            nc.vector.tensor_tensor(w_lo[:, s, :], raw[:, s, :], w_hi[:, s, :].bitcast(F32), ALU.subtract).then_inc(w_lo_done, 1)

        def x_low(hi, lo, k, base, g0):
            dve.wait_ge(xt_hi_done, base + k + 1)
            nc.vector.scalar_tensor_tensor(lo[:, k, :], x_bank(k, base)[:, :], gains[:, g0 + k:g0 + k + 1],
                                           hi[:, k, :].bitcast(F32), ALU.mult, ALU.subtract).then_inc(xt_lo_done, 1)

        def low_half(dst, src, hi, q, count, done):
            dve.wait_ge(q, count)
            nc.vector.tensor_tensor(dst, src, hi.bitcast(F32), ALU.subtract).then_inc(done, 1)

        def q_low(kind, src, q, count, done):
            dve.wait_ge(q, count)
            for h in range(2):
                own, other = slice(DH * h, DH * (h + 1)), slice(DH * (1 - h), DH * (2 - h))
                b = q_both[kind][h]
                nc.vector.tensor_tensor(b[other, :], src[own, :], b[own, :].bitcast(F32), ALU.subtract).then_inc(done, 1)

        def row_means(count):
            dve.wait_ge(sq_done, FIRST_SQ + 16 * (count - 1))
            nc.vector.tensor_reduce(total[:, :], sums[:, :, :], AX_X, ALU.add).then_inc(total_done, 1)
            dve.wait_ge(total_done, count)
            nc.vector.tensor_scalar(mean[:, 0:NT], total[:, :], 1.0 / D, EPS, ALU.mult, ALU.add).then_inc(mean_done, 1)

        def widen_r(wide, count, invs):
            dve.wait_ge(inv_done, invs)
            for t in range(NT):
                ins = nc.vector.tensor_scalar(wide[:, t, :], ones[:, :], inv[:, t:t + 1], None, ALU.mult)
            ins.then_inc(wide_done, 1)

        def take(dst, b, factor, used):
            dve.wait_ge(w_used, used)
            nc.vector.scalar_tensor_tensor(dst, bank[b][:, :], factor, r_bc[:, :], ALU.mult, ALU.mult).then_inc(acc_taken, 1)

        def set_bias(a, h):
            kind, odd, _ = HEAD[h]
            col = slope[:, bass.ds((0 if kind == "A" else HEADS) + 2 * a + odd, 1)]
            if kind == "A":
                nc.vector.scalar_tensor_tensor(bias[:, :], dist[:, :], col, lnm[:, :], ALU.mult, ALU.subtract).then_inc(bias_done, 1)
            else:
                nc.vector.tensor_scalar(bias[:, 0:2 * P], band[:, :], col, None, ALU.mult).then_inc(bias_done, 1)

        def lows(a, h, blocks, i0):
            kind = HEAD[h][0]
            if i0 == 0:
                dve.wait_ge(bias_done, 4 * a + h + 1)
            for i, (b, bk, c0, _, keys, _) in enumerate(blocks):
                dve.wait_ge(s_ready, 16 * a + 4 * h + i0 + with_bank(blocks, i))
                nc.vector.memset(tick[:, 4 * h + i0 + i:4 * h + i0 + i + 1], 0.0)
                s = bank[bk][:, c0:c0 + keys]
                end = SEQ if kind == "A" else 2 * P
                nc.vector.tensor_tensor_reduce(s, s, bias[:, end - keys:end], 1.0, FLOOR, ALU.add, ALU.min,
                                               low[:, 4 * h + b:4 * h + b + 1]).then_inc(low_done, 1)
            if kind == "B":
                dve.wait_ge(low_done, 16 * a + 4 * h + 4)
                four = low[:, 4 * h:4 * h + 4]
                nc.vector.tensor_scalar(four, four, neg_sink[:, bass.ds(2 * a + h - 2, 1)], None, ALU.min).then_inc(sunk, 1)

        def denominators(a, h):
            four = slice(4 * h, 4 * h + 4)
            dve.wait_ge(exp_done, 16 * a + 4 * h + 4)
            if h >= 2:
                dve.wait_ge(sink_done, 2 * a + h - 1)
                nc.vector.tensor_tensor(den[:, four], den[:, four], sink_exp[:, 4 * h - 8:4 * h - 4], ALU.add).then_inc(den_done, 1)
                dve.wait_ge(den_done, 2 * a + h - 1)
            nc.vector.reciprocal(inv_den[:, four], den[:, four]).then_inc(inv_den_done, 1)

        def pt_low(a, h, r):
            kind, _, r0 = HEAD[h]
            n = P * sum(len(q) for _, q, _ in (PT_A if kind == "A" else PT_B)[r])
            buf = (r0 + r) % 2
            low_half(pt_lo[:, buf, 0:n], bank[BANK_PT][:, 0:n], pt_hi[:, buf, 0:n], pt_hi_done, ROUNDS * a + r0 + r + 1, pt_lo_done)

        def take_o(a, h):
            odd = HEAD[h][1]
            own = slice(DH * odd, DH * (odd + 1))
            dve.wait_ge(o_low_done, 4 * a + h + 1)
            nc.vector.tensor_tensor(o_t[own, bass.ds(PAIRS * (h // 2) + a, 1), :].rearrange("p o c -> p (o c)"),
                                    bank[BANK_O][own, :], o_low[own, :], ALU.add).then_inc(o_taken, 1)

        def kv_low(kv):
            own, other = slice(DH * kv, DH * (kv + 1)), slice(DH * (1 - kv), DH * (2 - kv))
            low_half(k_lo["B"][own, :], kb_all[own, :], k_both["B"][0][own, :], kb_hi_done, 2 * kv + 2, kb_lo_done)
            dve.wait_ge(kb_lo_done, 2 * kv + 1)
            nc.vector.tensor_copy(k_lo["B"][other, :], k_lo["B"][own, :].bitcast(F32)).then_inc(kb_lo_done, 1)
            for h in range(2):
                low_half(v_both["B"][:, :, 1 + h, :], vb_all[:, :, own], v_both["B"][:, :, 3 * h, :], vb_hi_done, 2 * kv + h + 1, vb_lo_done)

        def attend(s, a):
            if s == 0:
                if not (isinstance(a, int) and a == 0):
                    take_o(a - 1, 3)
                set_bias(a, 0)
            if s == 1:
                lows(a, 0, S_A[:3], 0)
            if s == 2:
                lows(a, 0, S_A[3:], 3)
            if s == 3:
                denominators(a, 0)
                low_half(v_both["A"][:, :, 1:3, :], bank[BANK_O][:, :].rearrange("p (t h d) -> p t h d", h=2, d=DH),
                         v_both["A"][:, :, 0:4:3, :], va_hi_done, a + 1, va_lo_done)
                set_bias(a, 1)
            if s == 4:
                lows(a, 1, S_A[:3], 0)
            if s == 5:
                pt_low(a, 0, 0)
                lows(a, 1, S_A[3:], 3)
            if s == 6:
                denominators(a, 1)
                pt_low(a, 0, 1)
                set_bias(a, 2)
            if s == 7:
                pt_low(a, 0, 2)
                lows(a, 2, S_B, 0)
            if s == 8:
                take_o(a, 0)
                denominators(a, 2)
            if s in (9, 10, 11):
                pt_low(a, 1, s - 9)
            if s == 9:
                set_bias(a, 3)
            if s == 10:
                lows(a, 3, S_B, 0)
            if s == 12:
                denominators(a, 3)
                take_o(a, 1)
                pt_low(a, 2, 0)
            if s == 13:
                pt_low(a, 2, 1)
            if s == 15:
                take_o(a, 2)
            if s in (14, 15):
                pt_low(a, 3, s - 14)

        def pair(p, a):
            u = U_PAIR + 16 * p
            for s in range(16):
                split(*ahead(U_PAIR // 4 + 4 * p + s // 4, s % 4))
                if s == 0 and a is not None:
                    dve.wait_ge(ka_hi_done, 4 * p)
                    dve.wait_ge(ka_lo_done, 2 * p)
                    take(proj[1][:, :], BANK_K, -0.125, u)
                if s == 0 and a is None:
                    take(proj[0][:, :], BANK_K, 1.0, u)
                if s == 8:
                    take(proj[1][:, :], BANK_K, 1.0, u + 8)
                if a is not None:
                    attend(s, a)
                if s == 1 and a is not None:
                    q_low("B", proj[1], qb_hi_done, 2 * p, qb_lo_done)
                if s == 2 and a is None:
                    kv_low(0)
                if s == 4:
                    if a is None:
                        dve.wait_ge(vbt_ready, 1)
                    else:
                        dve.wait_ge(vt_ready, p)
                    take(proj[0][:, :], BANK_Q, -0.125, u + 4)
                if s == 6:
                    q_low("A", proj[0], qa_hi_done, 2 * (p + 1), qa_lo_done)
                if s == 9:
                    for h in range(2):
                        own = slice(DH * h, DH * (h + 1))
                        low_half(k_lo["A"][own, :], proj[1][own, :], k_both["A"][h][own, :], ka_hi_done,
                                 4 * p + h + 1, ka_lo_done)
                if s == 12:
                    take(proj[0][:, :], BANK_V, 1.0, u + 12)
                if s == 15 and a is None:
                    dve.wait_ge(gains_turned, 2)
                    nc.vector.tensor_copy(gains[:, KD:2 * KD + 2 * PAIRS], bank[BANK_PT][:, 0:KD + 2 * PAIRS]).then_inc(gains_done, 1)

        dve.wait_ge(gains_turned, 1)
        nc.vector.tensor_copy(gains[:, 0:KD], bank[BANK_Q][:, 0:KD]).then_inc(gains_done, 1)
        dve.wait_ge(gains_done, 1)
        for n in range(NC):
            for k in range(4 * n, 4 * n + 4):
                x_low(h_hi, h_lo, k, 0, G_ATTN)
            for u4, slot in START_SPLITS[n]:
                split(u4, slot)
        for t in range(NT):
            row = x_first[:, t, SEQ * (NC - 1):D]
            nc.vector.tensor_tensor_reduce(probs[1][:, SEQ:2 * SEQ], row, row, 1.0, 0.0, ALU.mult, ALU.add,
                                           sums[:, t, NC - 1:NC]).then_inc(sq_last_done, 1)
            dve.wait_ge(sq_last_done, t + 1)
        split(1, 2)
        dve.wait_ge(ones_done, 2)
        row_means(1)
        widen_r(squares[:, :].rearrange("p (t c) -> p t c", c=P), 1, 1)
        for s in range(4, 8):
            split(*ahead(1, s % 4))
            if s == 7:
                dve.wait_ge(rbc_ready, 1)
                nc.vector.tensor_copy(r_bc[:, :], bank[BANK_PT][:, :]).then_inc(rbc_done, 1)
                dve.wait_ge(rbc_done, 1)
                take(kb_all[:, :], BANK_Q, 1.0, 4)
        dve.wait_ge(consts_loaded, 16 * 5)
        nc.vector.tensor_scalar(neg_sink[:, :], sink[:, :], -1.0, None, ALU.mult).then_inc(neg_done, 1)
        dve.wait_ge(neg_done, 1)
        pair(0, None)
        pair(1, 0)
        with dve.Fori(2, 5) as p:
            pair(p, p - 1)
        kv_low(1)
        with dve.Fori(5, PAIRS) as p:
            pair(p, p - 1)

        def act_low(g, k):
            dve.wait_ge(act_hi_done, 4 * g + k + 1)
            nc.vector.scalar_tensor_tensor(act_lo[:, k, :], o_t[:, 4 * g + k, :],
                                           gains[:, G_OUT + 4 * g + k:G_OUT + 4 * g + k + 1],
                                           act_hi[:, k, :].bitcast(F32), ALU.mult, ALU.subtract).then_inc(act_lo_done, 1)

        def add_group(g, n, u4):
            cols = slice(512 * n, 512 * (n + 1))
            for t in range(NT):
                wait_group(dve, g, n, t, u4)
                b = group_bank(n, t, not isinstance(g, int) or g >= 4)[:, :]
                xt, yt = x_res[:, t, cols], y_a[:, t, cols]
                if isinstance(g, int) and g == 0:
                    nc.vector.tensor_copy(yt, b).then_inc(grp_taken, 1)
                elif isinstance(g, int) and g == 1:
                    nc.vector.tensor_tensor(yt, b, yt, ALU.add).then_inc(grp_taken, 1)
                elif isinstance(g, int) and g < 4:
                    nc.vector.scalar_tensor_tensor(xt, b, inv[:, 4 + t:5 + t], xt, ALU.mult, ALU.add).then_inc(grp_taken, 1)
                else:
                    nc.vector.tensor_tensor(xt, b, xt, ALU.add).then_inc(grp_taken, 1)

        def add_a(n):
            dve.wait_ge(inv_done, 2)
            dve.wait_ge(x_again[n], 16)
            dve.wait_ge(grp_taken, 16 + 4 * n + NT)
            for t in range(NT):
                xt = x_res[:, t, 512 * n:512 * (n + 1)]
                nc.vector.scalar_tensor_tensor(xt, y_a[:, t, 512 * n:512 * (n + 1)], inv[:, t:t + 1], xt,
                                               ALU.mult, ALU.add).then_inc(y_done, 1)

        for k in range(4):
            act_low(0, k)
        for g in range(4):
            u4 = U_OUT // 4 + 4 * g
            for s in range(16):
                split(*ahead(u4 + s // 4, s % 4))
                if g == 0:
                    if s == 0:
                        dve.wait_ge(ka_hi_done, 4 * PAIRS)
                        dve.wait_ge(ka_lo_done, 2 * PAIRS)
                        take(proj[1][:, :], BANK_K, -0.125, U_OUT)
                    attend(s, PAIRS - 1)
                    if s == 1:
                        q_low("B", proj[1], qb_hi_done, 2 * PAIRS, qb_lo_done)
                if g == 1 and s == 0:
                    take_o(PAIRS - 1, 3)
                if g == 1 and s == 3:
                    dve.wait_ge(ssq_ready, 1)
                    nc.vector.tensor_scalar(mean[:, :], bank[BANK_PT][:, 0:8], 1.0 / D_A, EPS, ALU.mult, ALU.add).then_inc(mean_done, 1)
                if s == 0 and g > 0:
                    act_low(g, 3)
                if s >= 13 and g < 3:
                    act_low(g + 1, s - 13)
                if g == 1 and s in (4, 8, 12):
                    add_a(s // 4 - 1)
                if g == 2 and s == 0:
                    add_a(NC - 1)
                    dve.wait_ge(y_done, 16)
                if s % 4 == 3 and not (g == 3 and s == 15):
                    add_group(g, s // 4, u4)
                if g == 3 and s > 4 and s % 4 == 3:
                    for k in range(s - 7, s - 3):
                        x_low(h2_hi, h2_lo, k, KD, G_FFN)
                if g == 3 and s == 15:
                    add_group(g, NC - 1, u4)

        def take_up(i, c, first):
            dve.wait_ge(w_used, U_FFN + 48 * i + 8 * (c + 1))
            nc.vector.tensor_tensor(up_s[:, :], bank[BANK_UP[c % 2]][:, :], r2_bc[:, :], ALU.mult).then_inc(gu_taken, 1)
            dve.wait_ge(gu_taken, 8 * i + 2 * c + 2)
            dve.wait_ge(silu_done, 4 * i + c + 1)
            if not (first and c == 0):
                dve.wait_ge(act_lo_done, 16 + 4 * i + c)
            nc.vector.tensor_tensor(act_s[:, :], up_s[:, :], silu_s[:, :], ALU.mult).then_inc(act_done, 1)

        def act_low_ffn(i, c):
            low_half(act_lo[:, c, :], act_s[:, :], act_hi[:, c, :], act_hi_done, 16 + 4 * i + c + 1, act_lo_done)

        def ffn(i, first, last):
            u = U_FFN + 48 * i
            for s in range(32 if last else 48):
                split(*ahead(U_FFN // 4 + 12 * i + s // 4, s % 4))
                if first and s == 2:
                    for k in range(12, KD):
                        x_low(h2_hi, h2_lo, k, KD, G_FFN)
                    row_means(2)
                    widen_r(r2_wide, 2, 3)
                if first and s == 4:
                    dve.wait_ge(rbc_ready, 2)
                    nc.vector.tensor_copy(r2_bc[:, :], bank[BANK_X[3]][:, :]).then_inc(rbc_done, 1)
                    dve.wait_ge(rbc_done, 2)
                if s < 32 and s % 8 == 4:
                    c = s // 8
                    dve.wait_ge(w_used, u + s)
                    if not (first and c == 0):
                        dve.wait_ge(silu_done, 4 * i + c)
                    nc.vector.tensor_tensor(gate_s[:, :], bank[BANK_GATE[c % 2]][:, :], r2_bc[:, :], ALU.mult).then_inc(gu_taken, 1)
                if s in (8, 16, 24, 32):
                    take_up(i, s // 8 - 1, first)
                if s in (9, 17, 25, 33):
                    act_low_ffn(i, s // 8 - 1)
                if s >= 32 and s % 4 == 3:
                    add_group(4 + i, (s - 32) // 4, u // 4 + 8)

        ffn(0, True, False)
        with dve.Fori(1, STEPS_F - 1) as i:
            ffn(i, False, False)
        ffn(STEPS_F - 1, False, True)
        last, u4 = STEPS_F - 1, U_FFN // 4 + 12 * STEPS_F - 4
        split(u4, AHEAD)
        take_up(last, 3, False)
        act_low_ffn(last, 3)
        dve.wait_ge(gfin_loaded, 16)

        def add_last(m):
            t, n = LAST[m]
            cols = slice(512 * n, 512 * (n + 1))
            dve.wait_ge(last_ready, m + 1)
            nc.vector.tensor_tensor(x_res[:, t, cols], bank[LAST_BANK[m % 8]][:, :], x_res[:, t, cols], ALU.add).then_inc(grp_taken, 1)
            if t == NT - 1:
                dve.wait_ge(grp_taken, 16 * (3 + STEPS_F) + m + 1)
                nc.vector.tensor_tensor(o_t[:, n, :], x_res[:, t, cols], g_fin[:, cols], ALU.mult).then_inc(gained, 1)

        def finish_mean(t, squares_done):
            dve.wait_ge(sq_done, FIRST_SQ + 16 + squares_done)
            nc.vector.tensor_reduce(total[:, t:t + 1], sums[:, t, :], AX_X, ALU.add).then_inc(total_done, 1)
            dve.wait_ge(total_done, 3 + t)
            nc.vector.tensor_scalar(mean[:, t:t + 1], total[:, t:t + 1], 1.0 / D, EPS, ALU.mult, ALU.add).then_inc(mean_done, 1)

        def finish_rows(t):
            dve.wait_ge(inv_done, 4 + t)
            nc.vector.scalar_tensor_tensor(x_res[:, t, :], x_res[:, t, :], inv[:, t:t + 1], g_fin[:, :],
                                           ALU.mult, ALU.mult).then_inc(scaled, 1)

        m = 0
        for j in range(4, 16):
            dve.wait_ge(w_hi_done, 4 * u4 + j + 1)
            nc.vector.tensor_tensor(h2_lo[:, j, :], raw[:, j % 4, :], h2_hi[:, j, :].bitcast(F32), ALU.subtract).then_inc(w_lo_done, 1)
            if j in (7, 11, 15):
                add_last(m)
                add_last(m + 1)
                m += 2
        add_last(6)
        add_last(7)
        finish_mean(0, 8)
        finish_mean(1, 8)
        add_last(8)
        add_last(9)
        finish_rows(0)
        add_last(10)
        add_last(11)
        finish_rows(1)
        finish_mean(2, 12)
        add_last(12)
        finish_rows(2)
        for m in range(13, 16):
            add_last(m)
        finish_mean(3, 16)
        dve.wait_ge(inv_done, 7)
        dve.wait_ge(gained, NC)
        nc.vector.tensor_scalar(x_res[:, NT - 1, 0:D // 2], o_t[:, 0:2, :].rearrange("p a c -> p (a c)"),
                                inv[:, NT - 1:NT], None, ALU.mult).then_inc(scaled, 1)

    @block.gpsimd
    def _(pool):
        def invert(count, cols):
            pool.wait_ge(mean_done, count)
            nc.gpsimd.tensor_tensor(inv[:, cols], mean[:, cols], half[:, cols], ALU.pow).then_inc(inv_done, 1)

        def scale_rows(a, h):
            pool.wait_ge(inv_den_done, 4 * a + h + 1)
            nc.gpsimd.tensor_tensor(tick[:, 16 + h:17 + h], half[:, 0:1], half[:, 0:1], ALU.add)
            for b, _, _, _, keys, e in (S_A if HEAD[h][0] == "A" else S_B):
                row = probs[h % 2][:, e:e + keys]
                nc.gpsimd.tensor_scalar(row, row, inv_den[:, 4 * h + b:4 * h + b + 1], 1.0, ALU.mult, ALU.mult).then_inc(p_ready, 1)

        def add_squares(a, j):
            s = sq_sum["AB"[j]][:, :]
            pool.wait_ge(o_sq_done, 2 * a + j + 1)
            nc.gpsimd.tensor_tensor(s, s, squares[:, :], ALU.add).then_inc(sq_added, 1)

        def attend(a):
            if not (isinstance(a, int) and a == 0):
                add_squares(a - 1, 1)
            scale_rows(a, 0)
            scale_rows(a, 1)
            scale_rows(a, 2)
            scale_rows(a, 3)
            add_squares(a, 0)

        nc.gpsimd.memset(ones[:, :], 1.0).then_inc(ones_done, 1)
        nc.gpsimd.memset(half[:, :], -0.5).then_inc(ones_done, 1)
        for kind in "AB":
            nc.gpsimd.memset(sq_sum[kind][:, :], 0.0).then_inc(zero_done, 1)
        pool.wait_ge(ones_done, 2)
        pool.wait_ge(zero_done, 2)
        invert(1, slice(0, NT))
        attend(0)
        with pool.Fori(1, PAIRS) as a:
            attend(a)
        add_squares(PAIRS - 1, 1)
        invert(2, slice(0, 2 * NT))
        invert(3, slice(0, NT))
        for t in range(NT):
            invert(4 + t, slice(t, t + 1))

    block.__exit__(None, None, None)


def constants():
    i = np.arange(P)[:, None]
    d = i + (SEQ - P) - np.arange(SEQ)[None, :]
    times = (d >= 0) * ((d <= 128) * 1 + (d % 4 == 0) + (d % 16 == 0))
    dist = np.where(times > 0, d, BIG).astype(np.float32)
    lnm = np.log(np.maximum(times, 1).astype(np.float64)).astype(np.float32)
    e = i + P - np.arange(2 * P)[None, :]
    band = np.where((e >= 0) & (e < WINDOW), e, BIG).astype(np.float32)
    idx = np.arange(2 * HEADS, dtype=np.float64)
    s = np.exp2(-8.0 * (idx + 1.0) / (2 * HEADS)).astype(np.float32)
    slope = np.tile(np.concatenate([s[0::2], s[1::2]])[None, :], (P, 1)).astype(np.float32)
    return {"c_dist": dist, "c_lnm": lnm, "c_band": band, "c_slope": np.ascontiguousarray(slope),
            "c_ident": np.eye(P, dtype=np.float32)}


INPUTS = ["x", "attn_norm", "w_in", "sinks", "out_norm_a", "out_norm_b", "w_out", "ffn_norm",
          "w_gate", "w_up", "w_down", "final_norm"]


def kernel(**inputs):
    import concourse.bacc as bacc
    from concourse.bass_utils import run_bass_kernel_spmd

    nc = bacc.Bacc("TRN2", target_bir_lowering=False, num_devices=1)
    arrays, args = {}, {}
    given = {name: np.ascontiguousarray(inputs[name]) for name in INPUTS}
    given.update(constants())
    for name, a in given.items():
        arrays[f"in_{name}"] = a
        args[name] = nc.dram_tensor(f"in_{name}", a.shape, mybir.dt.from_np(a.dtype), kind="ExternalInput").ap()
    args["out"] = nc.dram_tensor("out_x", (1, SEQ, D), F32, kind="ExternalOutput").ap()
    build(nc, **args)
    r = run_bass_kernel_spmd(nc, [arrays], core_ids=[0])
    return r.results[0]["out_x"]
```
